# Optimizing a Trainium2 kernel written in Bass

```python
import jax, jax.numpy as jnp
from jax import lax
import numpy as np

D_MODEL = 1024
BATCH = 1
SEQ = 1024
DEPTH = 2
DEC_BATCH = 8
DEC_SEQ = 1
PAST_LEN = 8192
PAGE_SIZE = 128

D_LRU = D_MODEL // 2
LRU_HEADS = 8
LRU_HD = D_LRU // LRU_HEADS
LRU_C = 8.0
CONV_W = 4
RET_HEADS = 4
RET_DK = D_MODEL // 16
RET_DV = 2 * RET_DK
D_RET = RET_HEADS * RET_DV
ROPE_BASE = 10000.0
SSD_HD = 64
D_SSD = D_MODEL // 2
SSD_HEADS = D_SSD // SSD_HD
SSD_GROUPS = 2
SSD_DSTATE = 128
SSD_CONV_DIM = D_SSD + 2 * SSD_GROUPS * SSD_DSTATE
D_MIX = D_LRU + D_RET + D_SSD
IN_SIZES = (D_LRU, D_LRU, RET_HEADS * RET_DK, RET_HEADS * RET_DK, D_RET, D_RET, D_SSD, SSD_CONV_DIM, SSD_HEADS)
D_IN = 2 * D_LRU + 2 * RET_HEADS * RET_DK + 2 * D_RET + D_SSD + SSD_CONV_DIM + SSD_HEADS
CHUNK = 128
D_FF = 128 * ((8 * D_MODEL // 3 + 127) // 128)
FFN_CONV_W = 3
EPS = 1e-6

kernel_name = 'hybrid_lru_retention_ssd_convffn_step'

def _rmsnorm(x, g):
    xf = x.astype(jnp.float32)
    y = xf * lax.rsqrt(jnp.mean(xf * xf, axis=-1, keepdims=True) + EPS)
    return (y * g.astype(jnp.float32)).astype(x.dtype)

def _split_cols(t, sizes):
    out, start = [], 0
    for s in sizes:
        out.append(t[..., start:start + s])
        start += s
    return out

def _chunk_len(L):
    return CHUNK if L % CHUNK == 0 else L

def _causal_dwconv(x, prev, w, b):
    W = w.shape[0]
    L = x.shape[1]
    xp = jnp.concatenate([prev.astype(x.dtype), x], axis=1)
    y = b
    for k in range(W):
        y = y + w[k] * xp[:, k:k + L]
    return y, xp[:, L:]

def _lin_combine(c1, c2):
    a1, b1 = c1
    a2, b2 = c2
    return a1 * a2, a2 * b1 + b2

def _rg_lru(xc, h0, wr, br, wi, bi, lam):
    f32 = jnp.float32
    bsz, L, _ = xc.shape
    xf = xc.astype(f32)
    xh = xf.reshape(bsz, L, LRU_HEADS, LRU_HD)
    r = jax.nn.sigmoid(jnp.einsum('blhi,hij->blhj', xh, wr.astype(f32)).reshape(bsz, L, D_LRU) + br.astype(f32))
    ig = jax.nn.sigmoid(jnp.einsum('blhi,hij->blhj', xh, wi.astype(f32)).reshape(bsz, L, D_LRU) + bi.astype(f32))
    log_a = -LRU_C * r * jax.nn.softplus(-lam.astype(f32))
    a = jnp.exp(log_a)
    b = jnp.sqrt(-jnp.expm1(2.0 * log_a)) * (ig * xf)
    b = b.at[:, 0].add(a[:, 0] * h0.astype(f32))
    _, h = lax.associative_scan(_lin_combine, (a, b), axis=1)
    return h, h[:, -1]

def _rotary(x, pos):
    half = x.shape[-1] // 2
    freqs = ROPE_BASE ** (-jnp.arange(half, dtype=jnp.float32) / half)
    ang = pos.astype(jnp.float32)[:, None] * freqs[None, :]
    cos = jnp.cos(ang)[None, :, None, :]
    sin = jnp.sin(ang)[None, :, None, :]
    xf = x.astype(jnp.float32)
    x1, x2 = xf[..., :half], xf[..., half:]
    return jnp.concatenate([x1 * cos - x2 * sin, x1 * sin + x2 * cos], axis=-1)

def _retention(q, k, v, s0):
    f32 = jnp.float32
    bsz, L, H, _ = q.shape
    C = _chunk_len(L)
    nc = L // C
    log_g = jnp.log1p(-jnp.exp2(-5.0 - jnp.arange(H, dtype=f32)))
    idx = jnp.arange(C, dtype=f32)
    diff = idx[:, None] - idx[None, :]
    decay = jnp.exp(jnp.where(diff[None] >= 0, diff[None] * log_g[:, None, None], -jnp.inf))
    q_dec = jnp.exp((idx[None, :] + 1.0) * log_g[:, None])[..., None]
    k_dec = jnp.exp((C - 1.0 - idx[None, :]) * log_g[:, None])[..., None]
    c_dec = jnp.exp(C * log_g)[:, None, None]

    def to_chunks(t):
        t = t.astype(f32).reshape(bsz, nc, C, H, t.shape[-1])
        return jnp.moveaxis(t, 1, 0).transpose(0, 1, 3, 2, 4)

    def step(s, inp):
        qb, kb, vb = inp
        scores = jnp.einsum('bhik,bhjk->bhij', qb, kb) * decay
        o = jnp.einsum('bhij,bhjv->bhiv', scores, vb) + jnp.einsum('bhik,bhkv->bhiv', qb * q_dec, s)
        s = s * c_dec + jnp.einsum('bhjk,bhjv->bhkv', kb * k_dec, vb)
        return s, o

    s, o = lax.scan(step, s0.astype(f32), (to_chunks(q), to_chunks(k), to_chunks(v)))
    o = o.transpose(1, 0, 3, 2, 4).reshape(bsz, L, H, v.shape[-1])
    return o, s

def _ssd(x, dt, a, bm, cm, s0):
    f32 = jnp.float32
    bsz, L = x.shape[:2]
    C = _chunk_len(L)
    nc = L // C
    R = SSD_HEADS // SSD_GROUPS
    mv = lambda t: jnp.moveaxis(t, 1, 0)
    xf = mv(x.astype(f32).reshape(bsz, nc, C, SSD_GROUPS, R, SSD_HD))
    dtf = dt.astype(f32).reshape(bsz, nc, C, SSD_GROUPS, R)
    daf = mv(dtf * a.astype(f32).reshape(SSD_GROUPS, R))
    dtf = mv(dtf)
    bf = mv(bm.astype(f32).reshape(bsz, nc, C, SSD_GROUPS, SSD_DSTATE))
    cf = mv(cm.astype(f32).reshape(bsz, nc, C, SSD_GROUPS, SSD_DSTATE))
    causal = jnp.tril(jnp.ones((C, C), dtype=bool))[None, :, :, None, None]

    def step(s, inp):
        xb, dtb, dab, bb, cb = inp
        cum = jnp.cumsum(dab, axis=1)
        seg = cum[:, :, None] - cum[:, None, :]
        lmask = jnp.exp(jnp.where(causal, seg, -jnp.inf))
        cbw = jnp.einsum('bign,bjgn->bijg', cb, bb)
        wgt = cbw[..., None] * lmask * dtb[:, None]
        y = jnp.einsum('bijgr,bjgrp->bigrp', wgt, xb)
        y = y + jnp.einsum('bign,bgrpn->bigrp', cb, s) * jnp.exp(cum)[..., None]
        wlast = jnp.exp(cum[:, -1:] - cum) * dtb
        s = s * jnp.exp(cum[:, -1])[..., None, None] + jnp.einsum('bjgr,bjgrp,bjgn->bgrpn', wlast, xb, bb)
        return s, y

    s0f = s0.astype(f32).reshape(bsz, SSD_GROUPS, R, SSD_HD, SSD_DSTATE)
    s, y = lax.scan(step, s0f, (xf, dtf, daf, bf, cf))
    y = jnp.moveaxis(y, 0, 1).reshape(bsz, L, SSD_HEADS, SSD_HD)
    return y, s.reshape(bsz, SSD_HEADS, SSD_HD, SSD_DSTATE)

def _layer_stack(x, pos, st_lru_conv, st_lru_h, st_ret, st_ssd_conv, st_ssd, st_ffn_conv, w):
    f32 = jnp.float32
    bsz, L, _ = x.shape
    refs = (st_lru_conv, st_lru_h, st_ret, st_ssd_conv, st_ssd, st_ffn_conv)
    new = [[] for _ in refs]
    for l in range(DEPTH):
        h = _rmsnorm(x, w['norm_mix_g'][l])
        proj = jnp.einsum('bld,de->ble', h, w['w_in'][l])
        lru_x, lru_gate, r_q, r_k, r_v, r_g, s_z, s_xbc, s_dt = _split_cols(proj, IN_SIZES)
        xc, lru_buf = _causal_dwconv(lru_x, st_lru_conv[l], w['lru_conv_w'][l], w['lru_conv_b'][l])
        h_lru, lru_last = _rg_lru(xc, st_lru_h[l], w['lru_wr'][l], w['lru_br'][l], w['lru_wi'][l], w['lru_bi'][l], w['lru_lambda'][l])
        y_a = h_lru.astype(x.dtype) * jax.nn.gelu(lru_gate)
        q = _rotary(r_q.reshape(bsz, L, RET_HEADS, RET_DK), pos)
        k = _rotary(r_k.reshape(bsz, L, RET_HEADS, RET_DK), pos) * (RET_DK ** -0.5)
        v = r_v.reshape(bsz, L, RET_HEADS, RET_DV)
        o, ret_last = _retention(q, k, v, st_ret[l])
        o = _rmsnorm(o, w['ret_norm_g'][l]).astype(x.dtype).reshape(bsz, L, D_RET)
        y_b = jax.nn.silu(r_g) * o
        xbc, ssd_buf = _causal_dwconv(s_xbc, st_ssd_conv[l], w['ssd_conv_w'][l], w['ssd_conv_b'][l])
        xbc = jax.nn.silu(xbc)
        xs, bm, cm = _split_cols(xbc, (D_SSD, SSD_GROUPS * SSD_DSTATE, SSD_GROUPS * SSD_DSTATE))
        dt = jax.nn.softplus(s_dt.astype(f32) + w['ssd_dt_bias'][l].astype(f32))
        a = -jnp.exp(w['ssd_a_log'][l].astype(f32))
        ys, ssd_last = _ssd(xs, dt, a, bm.reshape(bsz, L, SSD_GROUPS, SSD_DSTATE), cm.reshape(bsz, L, SSD_GROUPS, SSD_DSTATE), st_ssd[l])
        ys = ys + w['ssd_d'][l].astype(f32)[:, None] * xs.astype(f32).reshape(bsz, L, SSD_HEADS, SSD_HD)
        gated = ys * jax.nn.silu(s_z.astype(f32)).reshape(bsz, L, SSD_HEADS, SSD_HD)
        gated = gated.reshape(bsz, L, SSD_GROUPS, D_SSD // SSD_GROUPS)
        y_c = _rmsnorm(gated, w['ssd_norm_g'][l].reshape(SSD_GROUPS, D_SSD // SSD_GROUPS)).astype(x.dtype).reshape(bsz, L, D_SSD)
        mix = jnp.concatenate([y_a, y_b, y_c], axis=-1)
        x = x + jnp.einsum('blm,md->bld', mix, w['w_out'][l])
        h = _rmsnorm(x, w['norm_ffn_g'][l])
        gu = jnp.einsum('bld,df->blf', h, w['ffn_w_up'][l])
        gate, up = gu[..., :D_FF], gu[..., D_FF:]
        gate, ffn_buf = _causal_dwconv(gate, st_ffn_conv[l], w['ffn_conv_w'][l], w['ffn_conv_b'][l])
        x = x + jnp.einsum('blf,fd->bld', jax.nn.gelu(gate) * up, w['ffn_w_down'][l])
        for lst, val, ref in zip(new, (lru_buf, lru_last, ret_last, ssd_buf, ssd_last, ffn_buf), refs):
            lst.append(val.astype(ref.dtype))
    y = _rmsnorm(x, w['norm_final_g'])
    return y, [jnp.stack(s, axis=0) for s in new]

def setup_inputs(seed: int = 0) -> dict:
    key = jax.random.key(seed)
    ks = iter(jax.random.split(key, 48))
    f32 = jnp.float32

    def nrm(shape, scale):
        return jax.random.normal(next(ks), shape, f32) * scale

    x_prompt = nrm((BATCH, SEQ, D_MODEL), 1.0)
    x_sample = nrm((DEC_BATCH, DEC_SEQ, D_MODEL), 1.0)
    state_lru_conv = nrm((DEPTH, DEC_BATCH, CONV_W - 1, D_LRU), 1.0)
    state_lru_h = nrm((DEPTH, DEC_BATCH, D_LRU), 0.5)
    state_ret = nrm((DEPTH, DEC_BATCH, RET_HEADS, RET_DK, RET_DV), 0.5)
    state_ssd_conv = nrm((DEPTH, DEC_BATCH, CONV_W - 1, SSD_CONV_DIM), 1.0)
    state_ssd = nrm((DEPTH, DEC_BATCH, SSD_HEADS, SSD_HD, SSD_DSTATE), 0.1)
    state_ffn_conv = nrm((DEPTH, DEC_BATCH, FFN_CONV_W - 1, D_FF), 1.0)
    norm_mix_g = 1.0 + nrm((DEPTH, D_MODEL), 0.02)
    w_in = nrm((DEPTH, D_MODEL, D_IN), D_MODEL ** -0.5)
    lru_conv_w = nrm((DEPTH, CONV_W, D_LRU), CONV_W ** -0.5)
    lru_conv_b = nrm((DEPTH, D_LRU), 0.02)
    lru_wr = nrm((DEPTH, LRU_HEADS, LRU_HD, LRU_HD), LRU_HD ** -0.5)
    lru_br = nrm((DEPTH, D_LRU), 0.02)
    lru_wi = nrm((DEPTH, LRU_HEADS, LRU_HD, LRU_HD), LRU_HD ** -0.5)
    lru_bi = nrm((DEPTH, D_LRU), 0.02)
    a_lru = jax.random.uniform(next(ks), (DEPTH, D_LRU), f32, 0.9, 0.999)
    a_root = a_lru ** (1.0 / LRU_C)
    lru_lambda = jnp.log(a_root) - jnp.log1p(-a_root)
    ret_norm_g = 1.0 + nrm((DEPTH, RET_HEADS, RET_DV), 0.02)
    ssd_conv_w = nrm((DEPTH, CONV_W, SSD_CONV_DIM), CONV_W ** -0.5)
    ssd_conv_b = nrm((DEPTH, SSD_CONV_DIM), 0.02)
    dt0 = jnp.exp(jax.random.uniform(next(ks), (DEPTH, SSD_HEADS), f32, float(np.log(1e-3)), float(np.log(1e-1))))
    ssd_dt_bias = dt0 + jnp.log(-jnp.expm1(-dt0))
    ssd_a_log = jnp.log(jax.random.uniform(next(ks), (DEPTH, SSD_HEADS), f32, 1.0, 16.0))
    ssd_d = 1.0 + nrm((DEPTH, SSD_HEADS), 0.02)
    ssd_norm_g = 1.0 + nrm((DEPTH, D_SSD), 0.02)
    w_out = nrm((DEPTH, D_MIX, D_MODEL), D_MIX ** -0.5)
    norm_ffn_g = 1.0 + nrm((DEPTH, D_MODEL), 0.02)
    ffn_w_up = nrm((DEPTH, D_MODEL, 2 * D_FF), D_MODEL ** -0.5)
    ffn_conv_w = nrm((DEPTH, FFN_CONV_W, D_FF), FFN_CONV_W ** -0.5)
    ffn_conv_b = nrm((DEPTH, D_FF), 0.02)
    ffn_w_down = nrm((DEPTH, D_FF, D_MODEL), D_FF ** -0.5)
    norm_final_g = 1.0 + nrm((D_MODEL,), 0.02)
    return {'x_prompt': x_prompt, 'x_sample': x_sample,
            'state_lru_conv': state_lru_conv, 'state_lru_h': state_lru_h, 'state_ret': state_ret,
            'state_ssd_conv': state_ssd_conv, 'state_ssd': state_ssd, 'state_ffn_conv': state_ffn_conv,
            'norm_mix_g': norm_mix_g, 'w_in': w_in,
            'lru_conv_w': lru_conv_w, 'lru_conv_b': lru_conv_b, 'lru_wr': lru_wr, 'lru_br': lru_br,
            'lru_wi': lru_wi, 'lru_bi': lru_bi, 'lru_lambda': lru_lambda,
            'ret_norm_g': ret_norm_g,
            'ssd_conv_w': ssd_conv_w, 'ssd_conv_b': ssd_conv_b, 'ssd_dt_bias': ssd_dt_bias,
            'ssd_a_log': ssd_a_log, 'ssd_d': ssd_d, 'ssd_norm_g': ssd_norm_g,
            'w_out': w_out, 'norm_ffn_g': norm_ffn_g, 'ffn_w_up': ffn_w_up,
            'ffn_conv_w': ffn_conv_w, 'ffn_conv_b': ffn_conv_b, 'ffn_w_down': ffn_w_down,
            'norm_final_g': norm_final_g}

def reference(x_prompt, x_sample, state_lru_conv, state_lru_h, state_ret, state_ssd_conv, state_ssd, state_ffn_conv,
              norm_mix_g, w_in, lru_conv_w, lru_conv_b, lru_wr, lru_br, lru_wi, lru_bi, lru_lambda,
              ret_norm_g, ssd_conv_w, ssd_conv_b, ssd_dt_bias, ssd_a_log, ssd_d, ssd_norm_g,
              w_out, norm_ffn_g, ffn_w_up, ffn_conv_w, ffn_conv_b, ffn_w_down, norm_final_g):
    w = {'norm_mix_g': norm_mix_g, 'w_in': w_in, 'lru_conv_w': lru_conv_w, 'lru_conv_b': lru_conv_b,
         'lru_wr': lru_wr, 'lru_br': lru_br, 'lru_wi': lru_wi, 'lru_bi': lru_bi, 'lru_lambda': lru_lambda,
         'ret_norm_g': ret_norm_g, 'ssd_conv_w': ssd_conv_w, 'ssd_conv_b': ssd_conv_b,
         'ssd_dt_bias': ssd_dt_bias, 'ssd_a_log': ssd_a_log, 'ssd_d': ssd_d, 'ssd_norm_g': ssd_norm_g,
         'w_out': w_out, 'norm_ffn_g': norm_ffn_g, 'ffn_w_up': ffn_w_up, 'ffn_conv_w': ffn_conv_w,
         'ffn_conv_b': ffn_conv_b, 'ffn_w_down': ffn_w_down, 'norm_final_g': norm_final_g}
    bp = x_prompt.shape[0]
    p_lru_conv0 = jnp.zeros((DEPTH, bp) + state_lru_conv.shape[2:], state_lru_conv.dtype)
    p_lru_h0 = jnp.zeros((DEPTH, bp) + state_lru_h.shape[2:], state_lru_h.dtype)
    p_ret0 = jnp.zeros((DEPTH, bp) + state_ret.shape[2:], state_ret.dtype)
    p_ssd_conv0 = jnp.zeros((DEPTH, bp) + state_ssd_conv.shape[2:], state_ssd_conv.dtype)
    p_ssd0 = jnp.zeros((DEPTH, bp) + state_ssd.shape[2:], state_ssd.dtype)
    p_ffn_conv0 = jnp.zeros((DEPTH, bp) + state_ffn_conv.shape[2:], state_ffn_conv.dtype)
    pos_p = jnp.arange(x_prompt.shape[1], dtype=jnp.int32)
    pos_s = PAST_LEN + jnp.arange(x_sample.shape[1], dtype=jnp.int32)
    y_prompt, ns_p = _layer_stack(x_prompt, pos_p, p_lru_conv0, p_lru_h0, p_ret0, p_ssd_conv0, p_ssd0, p_ffn_conv0, w)
    y_sample, ns_s = _layer_stack(x_sample, pos_s, state_lru_conv, state_lru_h, state_ret, state_ssd_conv, state_ssd, state_ffn_conv, w)
    lru_conv_p, lru_h_p, ret_p, ssd_conv_p, ssd_p, ffn_conv_p = ns_p
    lru_conv_s, lru_h_s, ret_s, ssd_conv_s, ssd_s, ffn_conv_s = ns_s
    return (y_prompt, y_sample, lru_conv_p, lru_conv_s, lru_h_p, lru_h_s, ret_p, ret_s,
            ssd_conv_p, ssd_conv_s, ssd_p, ssd_s, ffn_conv_p, ffn_conv_s)


_drawn_inputs = setup_inputs


def setup_inputs(seed=0):
    import zlib

    import numpy as np

    out = dict(_drawn_inputs(seed))
    spreads = {}
    factors = {'lru_br': 8.0,
     'lru_bi': 7.606,
     'ret_norm_g': 6.44,
     'ssd_d': 4.843,
     'ssd_norm_g': 3.737,
     'ffn_conv_b': 4.077,
     'norm_final_g': 2.744}
    for name, (base, spread) in spreads.items():
        noise = np.random.default_rng([zlib.crc32(name.encode()), seed]).standard_normal(out[name].shape)
        drawn = base * np.exp(spread * noise) if base else spread * noise
        out[name] = __import__('jax').numpy.asarray(drawn.astype(out[name].dtype))
    for name, factor in factors.items():
        out[name] = (out[name] * factor).astype(out[name].dtype)
    return out
```

```python
from contextlib import ExitStack

import numpy as np

import concourse.bass as bass
from concourse import mybir

ALU = mybir.AluOpType
ACT = mybir.ActivationFunctionType
F32 = mybir.dt.float32
F32R = mybir.dt.float32r
AX_X = mybir.AxisListType.X

P = 128
D_MODEL, SEQ, DEPTH, DEC = 1024, 1024, 2, 8
PAST_LEN = 8192
T = SEQ + DEC
NG = 3
TG = T // NG
KD = D_MODEL // P
CHUNK = 128
NCH = SEQ // CHUNK
D_FF = 2816
FT = D_FF // P
FB = FT // 2
IN_TILES = 32
LRU_W, FFN_W = 4, 3
RET_H, RET_DK, RET_DV = 4, 64, 128
SSD_H = 8
EPS = 1e-6
SLOTS = IN_TILES + 12 + 6 * FB

_widths = [("lru_w", 16), ("lru_b", 4), ("br", 4), ("bi", 4), ("lam", 4), ("ret_g", 4),
           ("ssd_w", 32), ("ssd_b", 8), ("ssd_d", 4), ("ssd_g", 4), ("dt_bias", 8), ("a_log", 8),
           ("ffn_w", 66), ("ffn_b", 22), ("lru_h0", 32), ("lru_prev", 96), ("ssd_prev", 192),
           ("ffn_prev", 352), ("wdt", 64)]
COL, NPAR = {}, 0
for _n, _w in _widths:
    COL[_n] = NPAR
    NPAR += _w

_consts = [("ident", 128), ("causal", 128), ("decay", 512), ("sel", 1024), ("qdec", 256),
           ("kdec", 4), ("cdec", 2), ("gamma", 2)]
CON, NCON = {}, 0
for _n, _w in _consts:
    CON[_n] = NCON
    NCON += _w

UNITS = ["S0", "S1", "R0", "R1", "L0", "L1"]
TILE0 = {"S0": 0, "S1": 6, "R0": 12, "R1": 18, "L0": 24, "L1": 28}


def mains():
    def ins(a, b):
        return [("in", i) for i in range(a, b)]

    def out(u):
        return [("out", u, 0), ("out", u, 1)]
    first = ins(0, 6)
    rest = {
        0: ins(6, 14),
        1: ins(14, 16) + out(0) + ins(16, 20),
        2: ins(20, 22) + out(1) + ins(22, 26),
        3: ins(26, 28) + out(2) + ins(28, 32),
        4: out(3),
        5: out(4),
        6: out(5),
    }
    return first, rest


FIRST, REST = mains()
ORDER = FIRST + [m for u in range(7) for m in REST[u]]
assert len(ORDER) == 44


def ring_uses():
    at = {"norm": 0, "dt": 1}
    n = 2

    def main(m, n):
        if m[0] == "in":
            at[m] = n
            return n + 1
        for i in range(4):
            at[m + (i,)] = n + i
        return n + 4
    for m in FIRST:
        n = main(m, n)
    for u in range(7):
        for m in REST[u]:
            n = main(m, n)
        if u < 4:
            for i in range(1 if u < 2 else 2):
                at["norm", u, i] = n
                n += 1
    at["norm2"] = n
    return at, n + 1


RING, R0 = ring_uses()
RUSES = R0 + 12 * FB
FREE = 1


class Signals:

    def __init__(self, nc, ctx, before):
        self.nc, self.ctx, self.before = nc, ctx, before
        self.sems, self.count, self.at, self.delta = {}, {}, {}, {}
        self.loops, self.turns = [], {}

    def sem(self, kind):
        if kind not in self.sems:
            self.sems[kind] = self.ctx.enter_context(self.nc.semaphore(kind))
        return self.sems[kind]

    def on(self, kind, key=None, n=1):
        self.count[kind] = self.count.get(kind, 0) + n
        self.at[kind, key] = (self.count[kind], [x for x, _ in self.loops])
        return self.sem(kind), n

    def loop(self, name, turns, var):
        return _Loop(self, name, turns, var)

    def value(self, kind, key, last=False):
        src = self.before or self
        if (kind, key) not in src.at:
            assert self.before is None, (kind, key)
            return 1
        first, loops = src.at[kind, key]
        now = dict(self.loops)
        v = first
        for x in loops:
            step = src.delta.get((x, kind), 0)
            v = v + now[x] * step if x in now else v + (src.turns[x] - 1) * step
        return v

    def after(self, kind, key=None):
        return self.sem(kind), self.value(kind, key)


class Line:

    def __init__(self, sg, kind):
        self.sg, self.kind, self.n = sg, kind, 0

    def step(self):
        self.n += 1
        return self.sg.on(self.kind, self.n)

    def last(self):
        return self.sg.after(self.kind, self.n)


def pick(tile, base, blk, stride, off, n=1):
    if isinstance(blk, int):
        at = base + blk * stride + off
        return tile[:, at:at + n]
    return tile[:, bass.ds(blk * stride + (base + off), n)]


class _Loop:
    def __init__(self, s, name, turns, var):
        self.s, self.name, self.turns, self.var = s, name, turns, var

    def __enter__(self):
        self.s.loops.append((self.name, self.var))
        self.start = dict(self.s.count)
        return self.var

    def __exit__(self, *a):
        s = self.s
        s.loops.pop()
        s.turns[self.name] = self.turns
        for k, v in s.count.items():
            d = v - self.start.get(k, 0)
            if d:
                s.delta[self.name, k] = d
                s.count[k] = v + d * (self.turns - 1)


def build(nc, io, ctx, before):
    sg = Signals(nc, ctx, before)

    def sb(name, shape, dt=F32):
        return ctx.enter_context(nc.sbuf_tensor("sb_" + name, shape, dt))

    x = sb("x", [P, KD, T])
    h_hi = sb("h_hi", [P, KD, T], F32R)
    h_lo = sb("h_lo", [P, KD, T], F32R)
    w_raw = sb("w_raw", [P, 2, 1024])
    w_hi = sb("w_hi", [P, 2, 1024], F32R)
    w_lo = sb("w_lo", [P, 2, 1024], F32R)
    y_hi = sb("y_hi", [P, 2, T], F32R)
    y_lo = sb("y_lo", [P, 2, T], F32R)
    rstd = sb("rstd", [P, T])
    pt = sb("pt", [P, 6, T])
    raw = sb("raw", [P, 2, T + 3])
    ev = sb("ev", [P, 2, T])
    ch = sb("ch", [P, 2568])
    par = sb("par", [P, NPAR])
    gains = sb("gains", [P, (2 * DEPTH + 1) * KD])
    con = sb("con", [P, NCON])
    tok = sb("tok", [P, 5, 72])
    ones = sb("ones", [P, P])
    gate_w = sb("gate_w", [P, 4, P])
    wdt = sb("wdt", [P, 64])
    small = sb("small", [P, 64])
    rgc = sb("rgc", [P, 4, 6])
    ring = ctx.enter_context(nc.psum_tensor("ring", [P, 2, NG, 512], F32))
    ab = ctx.enter_context(nc.psum_tensor("ab", [P, 2, 512], F32))
    abf = ab[:].rearrange("p a n -> p (a n)")

    def C(name, i=0, n=1):
        return con[:, CON[name] + i:CON[name] + i + n]

    def A(name, i=0, n=1):
        return par[:, COL[name] + i:COL[name] + i + n]

    ident = C("ident", 0, 128)
    T0, T1 = ch[:, 0:T], ch[:, T:2 * T]
    Btok, xtok, xw, cbm = ch[:, 0:128], ch[:, 128:384], ch[:, 384:640], ch[:, 640:768]
    seg, Ec, Ce, St = ch[:, 768:1284], ch[:, 1284:1796], ch[:, 1796:2308], ch[:, 2308:2564]
    kd, qd, sT, vtok = Btok, cbm, xw, xtok

    def g3(ap):
        return ap.rearrange("p (g n) -> p g n", g=NG)

    def cols(c):
        return slice(c * CHUNK, (c + 1) * CHUNK)

    def freed(layer, r, base=0):
        return sg.sem("m_free"), layer * RUSES + base + (r + 1 + FREE)

    block = ctx.enter_context(nc.Block())

    class Ring:
        def __init__(self):
            self.r = 0

        def next(self):
            self.r += 1
            return self.r - 1

    @block.sync
    def _(sp):
        def step():
            sp.sem_inc(sg.sem("sync_steps"), 1)

        sp.dma_start(con[:], io["con"]).then_inc(*sg.on("const_loaded", None, 16))
        sp.dma_start(gains[:], io["gains"]).then_inc(*sg.on("gains_loaded", None, 16))
        for m in range(KD):
            sp.dma_start(x[:, m, :], io["x"][m]).then_inc(*sg.on(f"x_loaded{m}", None, 16))
        for name in ("lru", "ssd", "ffn"):
            sp.dma_start(io[f"o_{name}_old"], io[f"i_{name}_old"]).then_inc(*sg.on("old_rows", None, 16))

        def weights(s, first=False):
            sp.wait_ge(sg.sem("w_split_done"), layer * SLOTS + (max(s - 1, 0) + FREE))
            step()
            sp.dma_start(w_raw[:, s % 2, :], io["w"][layer * SLOTS + s]).then_inc(*sg.on(f"w_raw{s % 2}", s, 16))

        with sp.Fori(0, DEPTH) as layer, sg.loop("layer", DEPTH, layer):
            sp.wait_ge(sg.sem("par_free"), layer + FREE)
            step()
            sp.dma_start(par[:], io["par"][layer]).then_inc(*sg.on("par_loaded", None, 16))
            weights(0)
            weights(1)
            fill = [2]

            def more(upto):
                while fill[0] < min(upto, SLOTS):
                    weights(fill[0])
                    fill[0] += 1

            def spill(i):
                sp.wait_ge(*freed(layer, RING["in", i]))
                step()
                sp.dma_start(io["proj"][i], ev[:, i % 2, :]).then_inc(*sg.on(f"ev_stored{i % 2}", i, 16))

            def stored(i):
                sp.wait_ge(*sg.after(f"ev_stored{i % 2}", i))
                step()

            slot = [0]

            def main(m):
                more(slot[0] + 3)
                if m[0] == "in":
                    spill(m[1])
                slot[0] += 1

            def load_conv(u, j, tile):
                stored(tile)
                if j >= 2:
                    sp.wait_ge(*sg.after("conv_done", (u, j - 2)))
                    step()
                sp.dma_start(raw[:, j % 2, 3:T + 3],
                             io["proj"][tile]).then_inc(*sg.on("raw_loaded" + str(j % 2), (u, j), 16))

            def prep(u):
                t0 = TILE0[UNITS[u]]
                if u > 0:
                    sp.wait_ge(*sg.after("y_split", u - 1))
                    step()
                    sp.wait_ge(*sg.after("small_stored", (u - 1, 1)))
                    step()
                if u < 2:
                    for j in range(4):
                        load_conv(u, j, t0 + j)
                    for j in (4, 5):
                        stored(t0 + j)
                        sp.dma_start(pt[:, j, :], io["proj"][t0 + j]).then_inc(*sg.on("gate_loaded", (u, j), 16))
                elif u < 4:
                    for j in range(6):
                        stored(t0 + j)
                    sp.dma_start(T0, io["cos"]).then_inc(*sg.on("rope_loaded", (u, 0), 16))
                    sp.dma_start(T1, io["sin"]).then_inc(*sg.on("rope_loaded", (u, 1), 16))
                    for j in range(2):
                        sp.dma_start(pt[:, j, :], io["proj"][t0 + j]).then_inc(*sg.on("qk_loaded", (u, j), 16))
                        for q in range(4):
                            sp.dma_start(raw[32 * q:32 * q + 32, j, 0:T],
                                         io["proj"][t0 + j, 32 * (q ^ 1):32 * (q ^ 1) + 32, :]).then_inc(*sg.on("qk_loaded", (u, j, q), 16))
                    for j in range(2, 6):
                        sp.dma_start(pt[:, j, :], io["proj"][t0 + j]).then_inc(*sg.on("vg_loaded", (u, j), 16))
                else:
                    for j in range(2):
                        load_conv(u, j, t0 + j)
                    sp.dma_start(gate_w[:], io["gate_w"][layer, u - 4]).then_inc(*sg.on("gate_w_loaded", u, 16))
                    for j in (2, 3):
                        stored(t0 + j)
                        sp.wait_ge(*sg.after("conv_done", (u, j - 2)))
                        step()
                        sp.dma_start(raw[:, j - 2, 0:T],
                                     io["proj"][t0 + j]).then_inc(*sg.on("gate_loaded", (u, j), 16))

            def load_states(u):
                if u < 2:
                    sp.wait_ge(*sg.after("conv_done", (u, 3)))
                    step()
                    sp.wait_ge(*sg.after("conv_done", (u, 2)))
                    step()
                    rf = raw[:].rearrange("p a n -> p (a n)")[:, 0:2048].rearrange("p (a n) -> p a n", a=2)
                    sp.dma_start(rf, io["ssd_state"][layer, u]).then_inc(*sg.on("dec_loaded", u, 16))
                elif u < 4:
                    sp.wait_ge(*sg.after("rope_done", u))
                    step()
                    sp.dma_start(raw[:, 0, 0:1024],
                                 io["ret_state"][layer, u - 2]).then_inc(*sg.on("dec_loaded", u, 16))

            def finish(u):
                if u < 2:
                    rf = raw[:].rearrange("p a n -> p (a n)")[:, 0:2048].rearrange("p (a n) -> p a n", a=2)
                    sp.wait_ge(*sg.after("ab_free", (u, NCH)))
                    step()
                    sp.dma_start(io["o_ssd_p"][layer, u], St).then_inc(*sg.on("small_stored", (u, 0), 16))
                    sp.wait_ge(*sg.after("dec_state_done", u))
                    step()
                    sp.dma_start(io["o_ssd_s"][layer, u], rf).then_inc(*sg.on("small_stored", (u, 1), 16))
                elif u < 4:
                    rf = raw[:, 0, 0:1024]
                    sp.wait_ge(*sg.after("ab_free", (u, NCH)))
                    step()
                    sp.dma_start(io["o_ret_p"][layer, u - 2],
                                 St[:, 0:128]).then_inc(*sg.on("small_stored", (u, 0), 16))
                    sp.wait_ge(*sg.after("dec_state_done", u))
                    step()
                    sp.dma_start(io["o_ret_s"][layer, u - 2], rf).then_inc(*sg.on("small_stored", (u, 1), 16))
                else:
                    for j in range(2):
                        sp.wait_ge(*sg.after("h_done", (u, j)))
                        step()
                        sp.dma_start(io["o_lru_h"][layer, 2 * (u - 4) + j],
                                     pt[:, j, SEQ - 1:T]).then_inc(*sg.on("small_stored", (u, j), 16))

            for m in FIRST:
                main(m)
            for u in range(7):
                if u < 6:
                    prep(u)
                ms = list(REST[u])
                if u < 4:
                    for m in ms[:3]:
                        main(m)
                    load_states(u)
                    for m in ms[3:]:
                        main(m)
                    finish(u)
                elif u < 6:
                    for m in ms:
                        main(m)
                    finish(u)
                else:
                    for m in ms:
                        main(m)
            for i in range(IN_TILES):
                if i >= IN_TILES - 2:
                    stored(i)
            for j in range(2):
                sp.dma_start(io["o_ssd_new"][layer, 4 * j:4 * j + 4],
                             io["proj"][6 * j:6 * j + 4, :, SEQ - 3:T]).then_inc(*sg.on("rows_stored", j, 16))
                sp.dma_start(io["o_lru_new"][layer, 2 * j:2 * j + 2],
                             io["proj"][24 + 4 * j:26 + 4 * j, :, SEQ - 3:T]).then_inc(*sg.on("rows_stored", 2 + j, 16))

            s0 = 44
            for s in range(4):
                more(s0 + s + 3)

            sp.wait_ge(*sg.after("rows_stored", 3))
            step()
            for j in range(2):
                sp.wait_ge(*freed(layer, R0 + j))
                step()
                sp.dma_start(io["o_ffn_new"][layer, j],
                             raw[:, j, SEQ:T + 2]).then_inc(*sg.on(f"ffn_stored{j}", "first", 16))
            assert fill[0] == s0 + 6
            with sp.Fori(0, FB - 1) as b, sg.loop("ffn", FB - 1, b):
                for s in range(6):
                    sp.wait_ge(sg.sem("w_split_done"), layer * SLOTS + b * 6 + (s0 + 5 + s + FREE))
                    step()
                    sp.dma_start(w_raw[:, s % 2, :],
                                 io["w"][layer * SLOTS + b * 6 + (s0 + 6 + s)]).then_inc(*sg.on(f"w_raw{s % 2}", ("ffn", s), 16))
                    if s in (1, 3):
                        j = s // 2
                        sp.wait_ge(*freed(layer, R0 + 4 + j, b * 12))
                        step()
                        sp.dma_start(io["o_ffn_new"][layer, b * 2 + (2 + j)],
                                     raw[:, j, SEQ:T + 2]).then_inc(*sg.on(f"ffn_stored{j}", "loop", 16))
            for j in range(2):
                sp.wait_ge(sg.sem(f"ffn_stored{j}"), layer * (16 * FB) + 16 * FB)
                step()
        for m in range(KD):
            sp.wait_ge(*sg.after("y_ready", m))
            step()
            sp.dma_start(io["y"][m], ev[:, m % 2, :]).then_inc(*sg.on(f"y_stored{m % 2}", m, 16))
        for kind in ("old_rows", "small_stored", "rows_stored", "ffn_stored0", "ffn_stored1", "y_stored0", "y_stored1"):
            sp.wait_ge(sg.sem(kind), (before or sg).count.get(kind, 16))
            step()

    @block.gpsimd
    def _(pool):
        pool.wait_ge(*sg.after("ones_ready"))
        pool.nop().then_inc(sg.sem("w_split_done"), FREE)
        with pool.Fori(0, DEPTH) as layer, sg.loop("layer", DEPTH, layer):
            with pool.Fori(0, SLOTS // 2) as i, sg.loop("split", SLOTS // 2, i):
                for q in range(2):
                    n = layer * (SLOTS // 2) + i
                    pool.wait_ge(sg.sem(f"w_raw{q}"), n * 16 + 16)
                    pool.wait_ge(sg.sem(f"w_used{q}"), n + FREE)
                    nc.gpsimd.tensor_tensor(w_hi[:, q, :], w_raw[:, q, :], ones[:, 0:1].to_broadcast([P, 1024]),
                                            ALU.mult).then_inc(sg.sem("w_hi_done"), 1)
                    pool.wait_ge(sg.sem("w_hi_done"), n * 2 + (q + 1))
                    nc.gpsimd.tensor_tensor(w_lo[:, q, :], w_raw[:, q, :], w_hi[:, q, :].bitcast(F32),
                                                 ALU.subtract).then_inc(*sg.on("w_split_done", q))

    @block.tensor
    def _(pe):
        mm = nc.tensor.matmul

        used = []

        def free_used(base=0):
            if used:
                q, r = used.pop()
                pe.wait_ge(sg.sem("m_ready"), layer * RUSES + base + (r + 1))
                pe.nop().then_inc(sg.sem(f"w_used{q}"), 1)

        def three(out, wh, wl, ah, al, first, last):
            for g in range(NG):
                c = slice(g * TG, (g + 1) * TG)
                mm(out[:, g, 0:TG], wh, ah[:, c], start=first, stop=False)
                mm(out[:, g, 0:TG], wh, al[:, c], start=False, stop=False)
                ins = mm(out[:, g, 0:TG], wl, ah[:, c], start=False, stop=last)
            return ins

        rg = Ring()
        ready = {}
        slot = [0]

        def in_half(m, half):
            if half == 0:
                pe.wait_ge(sg.sem("w_split_done"), layer * SLOTS + (slot[0] + 1 + FREE))
                m_r[0] = rg.next()
                pe.wait_ge(sg.sem("m_free"), layer * RUSES + (max(m_r[0] - 1, 0) + FREE))
            q = slot[0] % 2
            out = ring[:, m_r[0] % 2]
            for k in range(4 * half, 4 * half + 4):
                ins = three(out, w_hi[:, q, k * P:(k + 1) * P], w_lo[:, q, k * P:(k + 1) * P],
                            h_hi[:, k, :], h_lo[:, k, :], k == 0, k == KD - 1)
                free_used()
            if half == 1:
                ins.then_inc(*sg.on("m_ready", m_r[0]))
                used.append((q, m_r[0]))
                slot[0] += 1

        m_r = [0]

        def out_half(m, half):
            if half == 0:
                pe.wait_ge(sg.sem("w_split_done"), layer * SLOTS + (slot[0] + 1 + FREE))
            q = slot[0] % 2
            for mm_ in range(2 * half, 2 * half + 2):
                m_r[0] = rg.next()
                pe.wait_ge(sg.sem("m_free"), layer * RUSES + (max(m_r[0] - 1, 0) + FREE))
                out = ring[:, m_r[0] % 2]
                for k in range(2):
                    c = slice((mm_ * 2 + k) * P, (mm_ * 2 + k + 1) * P)
                    ins = three(out, w_hi[:, q, c], w_lo[:, q, c], y_hi[:, k, :], y_lo[:, k, :], k == 0, k == 1)
                    free_used()
                ins.then_inc(*sg.on("m_ready", m_r[0]))
            if half == 1:
                used.append((q, m_r[0]))
                slot[0] += 1

        def main(m, half):
            if m is None:
                return
            if m[0] == "in":
                in_half(m, half)
            else:
                if m[2] == 0 and half == 0:
                    pe.wait_ge(*sg.after("y_split", m[1]))
                out_half(m, half)

        def both(m):
            main(m, 0)
            main(m, 1)

        def norm(key, tiles, wait_kind):
            r = rg.next()
            pe.wait_ge(sg.sem("m_free"), layer * RUSES + (max(r - 1, 0) + FREE))
            pe.wait_ge(*sg.after(wait_kind, key))
            for g in range(NG):
                for i, t in enumerate(tiles):
                    ins = mm(ring[:, r % 2, g, 0:TG], ones[:], t[:, g * TG:(g + 1) * TG],
                             start=i == 0, stop=i == len(tiles) - 1)
            ins.then_inc(*sg.on("m_ready", r))

        def ab_ready(u, c):
            if c > 0:
                pe.wait_ge(*sg.after("ab_free", (u, c)))
                return
            if u == 0:
                pe.wait_ge(*sg.after("cum_copied"))
            else:
                pe.wait_ge(*sg.after("gated", (u - 1, 1)))
            if u < 2:
                pe.wait_ge(*sg.after("silu", (u, 3)))
            else:
                pe.wait_ge(*sg.after("rope_done", u))
                pe.wait_ge(*sg.after("vg_loaded", (u, 5)))

        def stage1_s(u, c):
            ab_ready(u, c)
            s = cols(c)
            nc.tensor.transpose(ab[:, 0, 0:128], pt[:, 0, s], ident)
            nc.tensor.transpose(ab[:, 0, 128:256], pt[:, 2, s], ident)
            nc.tensor.transpose(ab[:, 0, 256:384], pt[:, 3, s], ident)
            mm(ab[:, 0, 384:512], pt[:, 0, s], pt[:, 1, s], start=True, stop=True)
            for h in range(4):
                da = tok[:, 1, 8 * c + 4 * u + h:8 * c + 4 * u + h + 1].to_broadcast([P, P])
                ins = mm(ab[:, 1, h * 128:(h + 1) * 128], da, C("causal", 0, 128), start=True, stop=True)
            ins.then_inc(*sg.on("stage1", (u, c)))

        def stage2_s(u, c):
            pe.wait_ge(*sg.after("mid_ready", (u, c)))
            for h in range(4):
                o = ab[64 * (h % 2):64 * (h % 2) + 64, 0, 128 * (h // 2):128 * (h // 2) + 128]
                mm(o, xtok[:, 64 * h:64 * h + 64], seg[:, 128 * h:128 * h + 128], start=True, stop=False)
                mm(o, St[:, 64 * h:64 * h + 64], Ce[:, 128 * h:128 * h + 128], start=False, stop=True)
            mm(ab[:, 0, 256:512], Btok, xw, start=True, stop=True).then_inc(*sg.on("stage2", (u, c)))

        def stage1_r(u, c):
            ab_ready(u, c)
            s = cols(c)
            nc.tensor.transpose(ab[:, 0, 0:128], pt[:, 2, s], ident)
            nc.tensor.transpose(ab[:, 0, 128:256], pt[:, 3, s], ident)
            nc.tensor.transpose(ab[:, 0, 256:384], pt[:, 1, s], ident)
            for h in range(2):
                r = slice(64 * h, 64 * h + 64)
                o = (ab[:, 1, 0:128], ab[:, 0, 384:512])[h]
                ins = mm(o, pt[r, 1, s], pt[r, 0, s], start=True, stop=True)
            ins.then_inc(*sg.on("stage1", (u, c)))

        def stage2_r(u, c):
            pe.wait_ge(*sg.after("mid_ready", (u, c)))
            for h in range(2):
                r = slice(64 * h, 64 * h + 64)
                o = ab[:, h, 0:128]
                mm(o, vtok[:, 128 * h:128 * h + 128], sT[:, 128 * h:128 * h + 128], start=True, stop=False)
                mm(o, St[r, 0:128], qd[r, :], start=False, stop=True)
            for h in range(2):
                ins = mm(ab[64 * h:64 * h + 64, 0, 256:384], kd[:, 64 * h:64 * h + 64],
                         vtok[:, 128 * h:128 * h + 128], start=True, stop=True)
            ins.then_inc(*sg.on("stage2", (u, c)))

        def decode_s(u):
            pe.wait_ge(*sg.after("ab_free", (u, NCH)))
            d = slice(SEQ, T)
            mm(ab[0:8, 0, 0:128], pt[:, 0, d], ident, start=True, stop=True)
            mm(ab[0:8, 0, 128:256], pt[:, 1, d], ident, start=True, stop=True)
            for w in range(2):
                for h in range(4):
                    v = tok[0:8, w, 64 + 4 * u + h:65 + 4 * u + h].to_broadcast([8, 64])
                    c0, r0 = 256 + 16 * w + 8 * (h // 2), 64 * (h % 2)
                    ins = mm(ab[r0:r0 + 64, 0, c0:c0 + 8], v, C("ident", 0, 8)[0:8], start=True, stop=True)
            ins.then_inc(*sg.on("dec_pe", (u, 0)))
            pe.wait_ge(*sg.after("dec_exp", u))
            for k in range(2):
                pe.wait_ge(*sg.after("dec_ready", (u, k)))
                for b in range(DEC):
                    ins = mm(abf[:, b * 128:(b + 1) * 128], C("sel", b * 128, 128)[0:8],
                             xtok[0:8, 128 * k:128 * k + 128], start=True, stop=True)
                ins.then_inc(*sg.on("dec_pe", (u, 1 + k)))

        def decode_r(u):
            pe.wait_ge(*sg.after("ab_free", (u, NCH)))
            d = slice(SEQ, T)
            mm(ab[0:8, 0, 0:128], pt[:, 2, d], ident, start=True, stop=True)
            mm(ab[0:8, 0, 128:256], pt[:, 3, d], ident, start=True, stop=True).then_inc(*sg.on("dec_pe", (u, 0)))
            pe.wait_ge(*sg.after("dec_ready", (u, 0)))
            for b in range(DEC):
                for h in range(2):
                    ins = mm(abf[64 * h:64 * h + 64, b * 128:(b + 1) * 128], C("sel", b * 128, 64)[0:8],
                             xtok[0:8, 128 * h:128 * h + 128], start=True, stop=True)
            ins.then_inc(*sg.on("dec_pe", (u, 1)))
            pe.wait_ge(*sg.after("dec_state_done", u))
            for h in range(2):
                for b in range(DEC):
                    r = slice(64 * h, 64 * h + 64)
                    ins = mm(ab[:, h, b:b + 1], raw[r, 0, b * 128:(b + 1) * 128],
                             pt[r, 0, SEQ + b:SEQ + b + 1], start=True, stop=True)
            ins.then_inc(*sg.on("dec_pe", (u, 2)))

        pe.wait_ge(*sg.after("const_loaded"))
        pe.wait_ge(*sg.after("ones_ready"))
        for q in range(2):
            pe.nop().then_inc(sg.sem(f"w_used{q}"), FREE)
        with pe.Fori(0, DEPTH) as layer, sg.loop("layer", DEPTH, layer):
            r = rg.next()
            pe.wait_ge(sg.sem("m_free"), layer * RUSES + (max(r - 1, 0) + FREE))
            pe.wait_ge(sg.sem("sq_summed"), 2 * layer + 1)
            for g in range(NG):
                ins = mm(ring[:, r % 2, g, 0:TG], ones[:], rstd[:, g * TG:(g + 1) * TG], start=True, stop=True)
            ins.then_inc(*sg.on("m_ready", r))
            r = rg.next()
            pe.wait_ge(sg.sem("m_free"), layer * RUSES + (max(r - 1, 0) + FREE))
            pe.wait_ge(*sg.after("wdt_ready"))
            for k in range(KD):
                for g in range(NG):
                    ins = mm(ring[0:8, r % 2, g, 0:TG], wdt[:, 8 * k:8 * k + 8], x[:, k, g * TG:(g + 1) * TG],
                             start=k == 0, stop=k == KD - 1)
            ins.then_inc(*sg.on("m_ready", r))
            both(FIRST[0])
            both(FIRST[1])
            pe.wait_ge(*freed(layer, RING["dt"]))
            for c in range(NCH):
                mm(ab[:, 0, 8 * c:8 * c + 8], pt[0:8, 0, cols(c)], ident[0:8, 0:8], start=True, stop=True)
            mm(ab[0:8, 0, 64:72], pt[0:8, 0, SEQ:T], ident[0:8, 0:8], start=True,
               stop=True).then_inc(*sg.on("dt_turned"))
            both(FIRST[2])
            pe.wait_ge(*sg.after("da_ready"))
            mm(ab[:, 0, 128:192], C("causal", 0, 128), tok[:, 1, 0:64], start=True,
               stop=True).then_inc(*sg.on("cum_done"))
            for m in FIRST[3:]:
                both(m)
            for u in range(4):
                s1, s2, dec = (stage1_s, stage2_s, decode_s) if u < 2 else (stage1_r, stage2_r, decode_r)
                ms = list(REST[u])
                both(ms.pop(0))
                for c in range(NCH):
                    m = ms.pop(0) if ms and c < 6 else None
                    s1(u, c)
                    main(m, 0)
                    s2(u, c)
                    main(m, 1)
                both(ms.pop(0))
                assert not ms
                dec(u)
                if u < 2:
                    norm((u, 0), [pt[:, 0, :], pt[:, 1, :]], "sq_ready")
                else:
                    norm((u, 0), [pt[:, 0, :]], "sq_ready")
                    norm((u, 1), [pt[:, 1, :]], "sq_ready")
            for u in range(4, 6):
                ms = list(REST[u])
                both(ms[0])
                pe.wait_ge(*sg.after("gate_w_loaded", u))
                for j in range(2):
                    pe.wait_ge(*sg.after("conv_done", (u, j)))
                    for g in range(NG):
                        if (j, g) != (0, 0):
                            pe.wait_ge(*sg.after("sig", (u, j, g - 1) if g else (u, j - 1, NG - 1)))
                        elif u == 4:
                            pe.wait_ge(*sg.after("gated", (3, 1)))
                        else:
                            pe.wait_ge(*sg.after("sig", (u - 1, 1, NG - 1)))
                        c = slice(g * TG, (g + 1) * TG)
                        mm(ab[:, 0, 0:TG], gate_w[:, 2 * j, :], pt[:, j, c], start=True, stop=True)
                        mm(ab[:, 1, 0:TG], gate_w[:, 2 * j + 1, :], pt[:, j, c], start=True,
                           stop=True).then_inc(*sg.on("gates", (u, j, g)))
                both(ms[1])
            for m in REST[6]:
                both(m)
            norm_r = rg.next()
            assert (norm_r, slot[0]) == (RING["norm2"], 44)
            pe.wait_ge(sg.sem("m_free"), layer * RUSES + (max(norm_r - 1, 0) + FREE))
            pe.wait_ge(sg.sem("sq_summed"), 2 * layer + 2)
            for g in range(NG):
                ins = mm(ring[:, norm_r % 2, g, 0:TG], ones[:], rstd[:, g * TG:(g + 1) * TG], start=True, stop=True)
            ins.then_inc(*sg.on("m_ready", norm_r))

            def ffn_slot(kind, q, r0, base, s, slot_base=0):
                pe.wait_ge(sg.sem("w_split_done"), layer * SLOTS + slot_base + (s + 1 + FREE))
                n = KD if kind == "up" else 2
                a, b_ = (h_hi, h_lo) if kind == "up" else (y_hi, y_lo)
                for i in range(1 if kind == "up" else 4):
                    r = r0 + i
                    pe.wait_ge(sg.sem("m_free"), layer * RUSES + base + (r - 1 + FREE))
                    for k in range(n):
                        c = slice((i * n + k) * P, (i * n + k + 1) * P)
                        ins = three(ring[:, r % 2], w_hi[:, q, c], w_lo[:, q, c], a[:, k, :], b_[:, k, :],
                                    k == 0, k == n - 1)
                        if i == k == 0:
                            pe.wait_ge(sg.sem("m_ready"), layer * RUSES + base + r0)
                            pe.nop().then_inc(sg.sem(f"w_used{1 - q}"), 1)
                    ins.then_inc(*sg.on("m_ready", ("ffn", r)))

            used.clear()
            for j in range(4):
                ffn_slot("up", j % 2, R0 + j, 0, 44 + j)
            with pe.Fori(0, FB - 1) as b, sg.loop("ffn", FB - 1, b):
                for j in range(4):
                    ffn_slot("up", j % 2, R0 + 4 + j, b * 12, 48 + j, b * 6)
                pe.wait_ge(sg.sem("ffn_split"), layer * FB + (b + 1))
                for j in range(2):
                    ffn_slot("down", j, R0 + 8 + 4 * j, b * 12, 52 + j, b * 6)
            pe.wait_ge(sg.sem("ffn_split"), layer * FB + FB)
            for j in range(2):
                ffn_slot("down", j, R0 + 4 + 4 * j, 12 * (FB - 1), 48 + j, 6 * (FB - 1))
            pe.wait_ge(sg.sem("m_ready"), layer * RUSES + RUSES)
            pe.nop().then_inc(sg.sem("w_used1"), 1)
        pe.wait_ge(sg.sem("sq_summed"), 2 * DEPTH + 1)
        pe.wait_ge(sg.sem("m_free"), DEPTH * RUSES + FREE)
        for g in range(NG):
            ins = mm(ring[:, 0, g, 0:TG], ones[:], rstd[:, g * TG:(g + 1) * TG], start=True, stop=True)
        ins.then_inc(*sg.on("last_sum"))

    @block.scalar
    def _(act):
        af = nc.scalar.activation
        line = Line(sg, "act_line")

        def conv_tap(u, j, dst, src, w, b):
            act.wait_ge(*sg.after(f"raw_loaded{j % 2}", (u, j)))
            af(dst, src, ACT.Identity, bias=b, scale=w).then_inc(*sg.on("tap", (u, j)))

        def refresh(m, g, key):
            if m >= 2:
                act.wait_ge(*sg.after("sq_used", (key, m - 2)))
            af(ev[:, m % 2, :], x[:, m, :], ACT.Square).then_inc(*sg.on("sq_tile", (key, m)))
            af(h_hi[:, m, :], x[:, m, :], ACT.Identity, scale=gains[:, bass.ds(g * KD + m, 1)]
                    if not isinstance(g, int) else gains[:, g * KD + m:g * KD + m + 1]).then_inc(*sg.on("h_hi", (key, m)))

        def root(r, t):
            act.wait_ge(*freed(layer, r))
            af(t, t, ACT.Sqrt).then_inc(*sg.on("root", r))

        def y_free(u):
            if u > 0:
                act.wait_ge(sg.sem("m_ready"), layer * RUSES + (RING["out", u - 1, 1, 3] + 1))

        act.wait_ge(*sg.after("gains_loaded"))
        for m in range(KD):
            act.wait_ge(*sg.after(f"x_loaded{m}"))
            refresh(m, 0, "start")
        with act.Fori(0, DEPTH) as layer, sg.loop("layer", DEPTH, layer):
            root(RING["norm"], rstd[:])
            act.wait_ge(*sg.after("par_loaded"))
            af(rgc[:, :, 0], A("lam", 0, 4), ACT.Abs).then_inc(*line.step())
            act.wait_ge(*line.last())
            af(rgc[:, :, 1], rgc[:, :, 0], ACT.Exp, scale=-1.0).then_inc(*sg.on("lam_exp"))
            af(small[:, 0:8], A("a_log", 0, 8), ACT.Exp).then_inc(*sg.on("a_exp"))
            act.wait_ge(*sg.after("dt_in"))
            af(tok[:, 3, :], tok[:, 2, :], ACT.Abs).then_inc(*line.step())
            act.wait_ge(*line.last())
            af(tok[:, 3, :], tok[:, 3, :], ACT.Exp, scale=-1.0).then_inc(*sg.on("dt_exp"))
            for u in range(2):
                for j in range(4):
                    t = 4 * u + j
                    if u == 0 and j == 0:
                        act.wait_ge(*sg.after("dt_turned"))
                    conv_tap(u, j, pt[:, j, :], raw[:, j % 2, 3:T + 3], A("ssd_w", 4 * t + 3), A("ssd_b", t))
                for j in range(4):
                    act.wait_ge(*sg.after("conv_done", (u, j)))
                    af(pt[:, j, :], pt[:, j, :], ACT.Silu).then_inc(*sg.on("silu", (u, j)))
                act.wait_ge(*sg.after("gate_loaded", (u, 5)))
                af(pt[:, 4:6, :], pt[:, 4:6, :], ACT.Silu).then_inc(*sg.on("gate_act", u))
                for c in range(NCH):
                    act.wait_ge(*sg.after("seg_ready", (u, c)))
                    af(Ec, ab[:, 1, :], ACT.Exp).then_inc(*sg.on("Ec_ready", (u, c)))
                    af(seg, seg, ACT.Exp).then_inc(*sg.on("seg_exp", (u, c)))
                act.wait_ge(*sg.after("dec_ready", (u, 0)))
                af(small[:, 16:32], ab[:, 0, 272:288], ACT.Exp).then_inc(*sg.on("dec_exp", u))
                for j in range(2):
                    act.wait_ge(*sg.after("gated", (u, j)))
                    af(pt[:, j, :], pt[:, 2 + j, :],
                       ACT.Square).then_inc(*sg.on("sq_ready", (u, 0) if j else (u, "a")))
                root(RING["norm", u, 0], pt[:, 4, :])
                for j in range(2):
                    act.wait_ge(*sg.after("y_done", (u, j)))
                    y_free(u)
                    af(y_hi[:, j, :], pt[:, 2 + j, :], ACT.Identity).then_inc(*sg.on("y_hi", (u, j)))
            for u in range(2, 4):
                act.wait_ge(*sg.after("vg_loaded", (u, 5)))
                af(pt[:, 4:6, :], pt[:, 4:6, :], ACT.Silu).then_inc(*sg.on("gate_act", u))
                act.wait_ge(*sg.after("gated", (u, 1)))
                for j in range(2):
                    af(pt[:, j, :], pt[:, 2 + j, :], ACT.Square).then_inc(*sg.on("sq_ready", (u, j)))
                for j in range(2):
                    root(RING["norm", u, j], (T0, T1)[j])
                for j in range(2):
                    act.wait_ge(*sg.after("y_done", (u, j)))
                    y_free(u)
                    af(y_hi[:, j, :], pt[:, 2 + j, :], ACT.Identity).then_inc(*sg.on("y_hi", (u, j)))
            for u in range(4, 6):
                for j in range(2):
                    t = 2 * (u - 4) + j
                    conv_tap(u, j, pt[:, j, :], raw[:, j, 3:T + 3], A("lru_w", 4 * t + 3), A("lru_b", t))
                for j in range(2):
                    t = 2 * (u - 4) + j
                    for g in range(NG):
                        c = slice(g * TG, (g + 1) * TG)
                        act.wait_ge(*sg.after("gates", (u, j, g)))
                        af(pt[:, 2 + j, c], ab[:, 0, 0:TG], ACT.Sigmoid, bias=A("br", t))
                        af(pt[:, 4 + j, c], ab[:, 1, 0:TG], ACT.Sigmoid,
                           bias=A("bi", t)).then_inc(*sg.on("sig", (u, j, g)))
                act.wait_ge(*sg.after("lam_ready"))
                act.wait_ge(*sg.after("sig", (u, 1, 2)))
                for j in range(2):
                    t = 2 * (u - 4) + j
                    af((T0, T1)[j], pt[:, 2 + j, :], ACT.Tanh, scale=rgc[:, t, 3:4]).then_inc(*sg.on("tanh", (u, j)))
                    act.wait_ge(*sg.after("tanh", (u, j)))
                    af(pt[:, 2 + j, :], pt[:, 2 + j, :], ACT.Exp,
                       scale=rgc[:, t, 4:5]).then_inc(*sg.on("a_done", (u, j)))
                for j in range(2):
                    act.wait_ge(*sg.after("e_done", (u, j)))
                    af((T0, T1)[j], (T0, T1)[j], ACT.Sqrt).then_inc(*sg.on("lru_root", (u, j)))
                act.wait_ge(*sg.after("gate_loaded", (u, 3)))
                for j in range(2):
                    af(raw[:, j, 0:T], raw[:, j, 0:T], ACT.Gelu_apprx_tanh).then_inc(*sg.on("gelu", (u, j)))
                for j in range(2):
                    act.wait_ge(*sg.after("y_done", (u, j)))
                    y_free(u)
                    af(y_hi[:, j, :], pt[:, 4 + j, :], ACT.Identity).then_inc(*sg.on("y_hi", (u, j)))
            for q in range(2):
                act.wait_ge(*sg.after(f"ev_stored{q}", IN_TILES - 2 + q))
            for m in range(KD):
                act.wait_ge(*freed(layer, RING["out", 5, m // 4, m % 4]))
                refresh(m, layer * 2 + 1, "ffn")
            root(RING["norm2"], rstd[:])

            def ffn_block(blk, tag, base):
                for j in range(2):
                    act.wait_ge(*freed(layer, R0 + j, base))
                    wt = A_dyn(blk, j)
                    af(pt[:, j, :], raw[:, j, 2:T + 2], ACT.Identity, bias=wt[3],
                       scale=wt[2]).then_inc(*sg.on("ffn_tap", (tag, j)))
                for j in range(2):
                    act.wait_ge(*sg.after("ffn_conv", (tag, j)))
                    af(pt[:, j, :], pt[:, j, :], ACT.Gelu_apprx_tanh).then_inc(*sg.on("ffn_gelu", (tag, j)))
                for j in range(2):
                    act.wait_ge(*sg.after("ffn_y", (tag, j)))
                    af(y_hi[:, j, :], pt[:, 2 + j, :], ACT.Identity).then_inc(*sg.on("ffn_hi", (tag, j)))

            def A_dyn(blk, j):
                base = COL["ffn_w"]
                out = []
                for k in range(3):
                    out.append(pick(par, base, blk, 6, 3 * j + k))
                out.append(pick(par, COL["ffn_b"], blk, 2, j))
                return out

            ffn_block(0, "first", 0)
            with act.Fori(0, FB - 1) as b, sg.loop("ffn", FB - 1, b):
                ffn_block(b + 1, "loop", b * 12 + 4)
            for m in range(KD):
                act.wait_ge(*freed(layer, R0 + 4 + m, 12 * (FB - 1)))
                refresh(m, layer * 2 + 2, "next")
        act.wait_ge(*sg.after("last_ms"))
        af(rstd[:], rstd[:], ACT.Sqrt).then_inc(*sg.on("last_root"))

    @block.vector
    def _(dve):
        v = nc.vector
        line = Line(sg, "dve_line")
        stt = v.scalar_tensor_tensor
        rg = Ring()

        def refresh(m, g, key):
            dve.wait_ge(*sg.after("sq_tile", (key, m)))
            if m == 0:
                v.tensor_copy(rstd[:], ev[:, 0, :]).then_inc(*sg.on("sq_used", (key, 0)))
            else:
                dve.wait_ge(*sg.after("sq_used", (key, m - 1)))
                v.tensor_tensor(rstd[:], rstd[:], ev[:, m % 2, :], ALU.add).then_inc(*sg.on("sq_used", (key, m)))
            dve.wait_ge(*sg.after("h_hi", (key, m)))
            gp = gains[:, bass.ds(g * KD + m, 1)] if not isinstance(g, int) else gains[:, g * KD + m:g * KD + m + 1]
            ins = stt(h_lo[:, m, :], x[:, m, :], gp, h_hi[:, m, :].bitcast(F32), ALU.mult, ALU.subtract)
            if m == KD - 1:
                ins.then_inc(sg.sem("sq_summed"), 1)

        def mean_square(dst, n, name):
            r = rg.next()
            assert r == RING[name]
            dve.wait_ge(sg.sem("m_ready"), layer * RUSES + (r + 1))
            v.tensor_scalar(g3(dst), ring[:, r % 2, :, 0:TG], 1.0 / n, EPS,
                            ALU.mult, ALU.add).then_inc(*sg.on("m_free", r))

        def root_inv(dst, name):
            dve.wait_ge(*sg.after("root", RING[name]))
            v.reciprocal(dst, dst).then_inc(*line.step())
            dve.wait_ge(*line.last())

        def conv(u, j, dst, src, w, prev, ntap):
            dve.wait_ge(*sg.after("tap", (u, j)))
            for k in range(ntap - 1):
                stt(dst[:, 0:SEQ], src[:, k:k + SEQ], w(k), dst[:, 0:SEQ], ALU.mult, ALU.add).then_inc(*line.step())
                dve.wait_ge(*line.last())
                ins = stt(dst[:, SEQ:T], prev(k), w(k), dst[:, SEQ:T], ALU.mult, ALU.add)
                if k < ntap - 2:
                    ins.then_inc(*line.step())
                    dve.wait_ge(*line.last())
            return ins

        def main(m, half, slotno=None):
            if m is None:
                return
            if m[0] == "in":
                if half == 1:
                    i = m[1]
                    r = rg.next()
                    dve.wait_ge(sg.sem("m_ready"), layer * RUSES + (r + 1))
                    if i >= 2:
                        dve.wait_ge(*sg.after(f"ev_stored{i % 2}", i - 2))
                    v.tensor_tensor(g3(ev[:, i % 2, :]), ring[:, r % 2, :, 0:TG], g3(rstd[:]),
                                    ALU.mult).then_inc(*sg.on("m_free", r))
            else:
                for i in range(2 * half, 2 * half + 2):
                    r = rg.next()
                    dve.wait_ge(sg.sem("m_ready"), layer * RUSES + (r + 1))
                    mo = 4 * m[2] + i
                    v.tensor_tensor(g3(x[:, mo, :]), ring[:, r % 2, :, 0:TG], g3(x[:, mo, :]),
                                    ALU.add).then_inc(*sg.on("m_free", r))
                    if m[1] == 5:
                        if mo > 0:
                            refresh(mo - 1, layer * 2 + 1, "ffn")
                        dve.wait_ge(*freed(layer, r))

        def both(m):
            main(m, 0)
            main(m, 1)

        v.memset(ones[:], 1.0).then_inc(*sg.on("ones_ready"))
        v.nop().then_inc(sg.sem("m_free"), FREE)
        v.nop().then_inc(sg.sem("par_free"), FREE)
        dve.wait_ge(*sg.after("gains_loaded"))
        dve.wait_ge(*sg.after("const_loaded"))
        for m in range(KD):
            dve.wait_ge(*sg.after(f"x_loaded{m}"))
            refresh(m, 0, "start")
        with dve.Fori(0, DEPTH) as layer, sg.loop("layer", DEPTH, layer):
            dve.wait_ge(*sg.after("par_loaded"))
            v.tensor_tensor(wdt[:].rearrange("p (k h) -> p k h", h=SSD_H),
                                 A("wdt", 0, 64).rearrange("p (k h) -> p k h", h=SSD_H),
                                 gains[:, bass.ds(layer * (2 * KD), KD)].unsqueeze(2).to_broadcast([P, KD, SSD_H]),
                                 ALU.mult).then_inc(*sg.on("wdt_ready"))
            mean_square(rstd[:], D_MODEL, "norm")
            root_inv(rstd[:], "norm")
            r = rg.next()
            dve.wait_ge(sg.sem("m_ready"), layer * RUSES + (r + 1))
            v.tensor_tensor(g3(pt[0:8, 0, :]), ring[0:8, r % 2, :, 0:TG], g3(rstd[0:8, :]),
                            ALU.mult).then_inc(*sg.on("m_free", r))
            both(FIRST[0])
            both(FIRST[1])

            def log1p(e, s, s2, p):
                v.tensor_scalar(s, e, 2.0, None, ALU.add).then_inc(*line.step())
                dve.wait_ge(*line.last())
                v.reciprocal(s, s).then_inc(*line.step())
                dve.wait_ge(*line.last())
                v.tensor_tensor(s, s, e, ALU.mult).then_inc(*line.step())
                dve.wait_ge(*line.last())
                v.tensor_tensor(s2, s, s, ALU.mult).then_inc(*line.step())
                dve.wait_ge(*line.last())
                v.tensor_scalar(p, s2, 1.0 / 17, None, ALU.mult).then_inc(*line.step())
                dve.wait_ge(*line.last())
                for n in (15, 13, 11, 9, 7, 5, 3):
                    stt(p, p, 1.0 / n, s2, ALU.add, ALU.mult).then_inc(*line.step())
                    dve.wait_ge(*line.last())
                stt(p, p, 1.0, s, ALU.add, ALU.mult).then_inc(*line.step())
                dve.wait_ge(*line.last())
                v.tensor_scalar(p, p, 2.0, None, ALU.mult).then_inc(*line.step())
                dve.wait_ge(*line.last())

            dve.wait_ge(*sg.after("lam_exp"))
            log1p(rgc[:, :, 1], rgc[:, :, 2], rgc[:, :, 3], rgc[:, :, 4])
            v.tensor_scalar(rgc[:, :, 2], A("lam", 0, 4), -1.0, 0.0, ALU.mult, ALU.max).then_inc(*line.step())
            dve.wait_ge(*line.last())
            v.tensor_tensor(rgc[:, :, 2], rgc[:, :, 2], rgc[:, :, 4], ALU.add).then_inc(*line.step())
            dve.wait_ge(*line.last())
            v.tensor_scalar(rgc[:, :, 3], rgc[:, :, 2], 8.0, None, ALU.mult).then_inc(*line.step())
            dve.wait_ge(*line.last())
            v.tensor_scalar(rgc[:, :, 4], rgc[:, :, 2], -8.0, None, ALU.mult).then_inc(*sg.on("lam_ready"))
            dve.wait_ge(*sg.after("dt_turned"))
            v.memset(tok[:, 2, :], 0.0).then_inc(*line.step())
            dve.wait_ge(*line.last())
            bias = A("dt_bias", 0, 8)
            v.tensor_tensor(tok[:, 2, 0:64].rearrange("p (c h) -> p c h", h=8),
                                 ab[:, 0, 0:64].rearrange("p (c h) -> p c h", h=8),
                                 bias.unsqueeze(1).to_broadcast([P, 8, 8]), ALU.add).then_inc(*line.step())
            dve.wait_ge(*line.last())
            v.tensor_tensor(tok[0:8, 2, 64:72], ab[0:8, 0, 64:72], bias[0:8], ALU.add).then_inc(*sg.on("dt_in"))
            dve.wait_ge(*sg.after("dt_exp"))
            log1p(tok[:, 3, :], tok[:, 1, :], tok[:, 4, :], tok[:, 0, :])
            v.tensor_scalar(tok[:, 2, :], tok[:, 2, :], 0.0, None, ALU.max).then_inc(*line.step())
            dve.wait_ge(*line.last())
            v.tensor_tensor(tok[:, 0, :], tok[:, 0, :], tok[:, 2, :], ALU.add).then_inc(*line.step())
            dve.wait_ge(*line.last())
            dve.wait_ge(*sg.after("a_exp"))
            stt(tok[:, 1, :].rearrange("p (c h) -> p c h", h=8), tok[:, 0, :].rearrange("p (c h) -> p c h", h=8),
                     -1.0, small[:, 0:8].unsqueeze(1).to_broadcast([P, 9, 8]), ALU.mult, ALU.mult).then_inc(*sg.on("da_ready"))
            both(FIRST[2])
            dve.wait_ge(*sg.after("cum_done"))
            v.tensor_copy(tok[:, 2, 0:64], ab[:, 0, 128:192]).then_inc(*sg.on("cum_copied"))
            for m in FIRST[3:]:
                both(m)

            def split(u, j, src):
                dve.wait_ge(*sg.after("y_hi", (u, j)))
                ins = v.tensor_tensor(y_lo[:, j, :], src, y_hi[:, j, :].bitcast(F32), ALU.subtract)
                if j == 1:
                    ins.then_inc(*sg.on("y_split", u))

            for u in range(4):
                ms = list(REST[u])
                both_first = ms.pop(0)
                hs = 4 * u
                if u < 2:
                    for j in range(2):
                        if u > 0:
                            pass
                        dve.wait_ge(*sg.after(f"raw_loaded{j}", (u, j)))
                        v.memset(raw[:, j, 0:3], 0.0).then_inc(*line.step())
                        dve.wait_ge(*line.last())
                    for j in range(4):
                        t = 4 * u + j
                        ins = conv(u, j, pt[:, j, :], raw[:, j % 2, :], lambda k: A("ssd_w", 4 * t + k),
                                   lambda k: A("ssd_prev", 24 * t + 8 * k, 8), LRU_W)
                        ins.then_inc(*sg.on("conv_done", (u, j)))
                        if j == 1:
                            both(both_first)
                    dve.wait_ge(*sg.after("silu", (u, 3)))
                    v.memset(St, 0.0).then_inc(*line.step())
                    dve.wait_ge(*line.last())
                else:
                    dve.wait_ge(*sg.after("rope_loaded", (u, 1)))
                    for j in range(2):
                        dve.wait_ge(*sg.after("qk_loaded", (u, 1, 3)))
                        sc = 1.0 if j == 0 else RET_DK ** -0.5
                        stt(raw[:, j, 0:T], raw[:, j, 0:T], sc, T1, ALU.mult, ALU.mult)
                        stt(pt[:, j, :], pt[:, j, :], sc, T0, ALU.mult, ALU.mult).then_inc(*line.step())
                        dve.wait_ge(*line.last())
                        ins = v.tensor_tensor(pt[:, j, :], pt[:, j, :], raw[:, j, 0:T], ALU.add)
                        if j == 0:
                            ins.then_inc(*line.step())
                            dve.wait_ge(*line.last())
                            both(both_first)
                        else:
                            ins.then_inc(*sg.on("rope_done", u))
                            dve.wait_ge(*sg.after("rope_done", u))
                    v.memset(St[:, 0:128], 0.0).then_inc(*line.step())
                    dve.wait_ge(*line.last())
                    dve.wait_ge(*sg.after("vg_loaded", (u, 5)))
                for c in range(NCH):
                    m = ms.pop(0) if ms and c < 6 else None
                    s = cols(c)
                    dve.wait_ge(*sg.after("stage1", (u, c)))
                    if u < 2:
                        ct = tok[:, 2, 8 * c + 4 * u:8 * c + 4 * u + 4]
                        dtt = tok[:, 0, 8 * c + 4 * u:8 * c + 4 * u + 4]
                        bb = ab[:, 1, :].rearrange("p (h i) -> p h i", h=4)
                        v.tensor_tensor(seg[:, 512:516], bb[:, :, 127], ct, ALU.subtract)
                        for h in range(4):
                            ins = v.tensor_scalar(seg[:, 128 * h:128 * h + 128], bb[:, h, :], ct[:, h:h + 1], 0.0,
                                                  ALU.subtract, ALU.min)
                        ins.then_inc(*sg.on("seg_ready", (u, c)))
                        v.tensor_copy(ch[:, 0:384], ab[:, 0, 0:384])
                        v.tensor_tensor(cbm, ab[:, 0, 384:512], C("causal", 0, 128), ALU.mult).then_inc(*line.step())
                        dve.wait_ge(*line.last())
                        dve.wait_ge(*sg.after("Ec_ready", (u, c)))
                        v.tensor_tensor(Ce.rearrange("p (h i) -> p h i", h=4), Ec.rearrange("p (h i) -> p h i", h=4),
                                        pt[:, 1, s].unsqueeze(1).to_broadcast([P, 4, 128]), ALU.mult)
                        dve.wait_ge(*sg.after("seg_exp", (u, c)))
                        v.tensor_tensor(seg[:, 512:516], seg[:, 512:516], dtt, ALU.mult).then_inc(*line.step())
                        dve.wait_ge(*line.last())
                        v.tensor_tensor(xw.rearrange("p (h d) -> p h d", h=4), xtok.rearrange("p (h d) -> p h d", h=4),
                                        seg[:, 512:516].unsqueeze(2).to_broadcast([P, 4, 64]), ALU.mult)
                        for h in range(4):
                            e = seg[:, 128 * h:128 * h + 128]
                            ins = stt(e, e, dtt[:, h:h + 1], cbm, ALU.mult, ALU.mult)
                        ins.then_inc(*sg.on("mid_ready", (u, c)))
                        main(m, 0)
                        dve.wait_ge(*sg.after("stage2", (u, c)))
                        for j in range(2):
                            ins = stt(pt[:, 2 + j, s], pt[:, 2 + j, s], A("ssd_d", 2 * u + j),
                                      ab[:, 0, 128 * j:128 * j + 128], ALU.mult, ALU.add)
                        s4 = St.rearrange("p (h d) -> p h d", h=4)
                        el = Ec.rearrange("p (h i) -> p h i", h=4)[:, :, 127:128].to_broadcast([P, 4, 64])
                        v.tensor_tensor(s4, s4, el, ALU.mult).then_inc(*line.step())
                        dve.wait_ge(*line.last())
                        v.tensor_tensor(St, St, ab[:, 0, 256:512], ALU.add).then_inc(*sg.on("ab_free", (u, c + 1)))
                    else:
                        g = u - 2
                        v.tensor_copy(vtok, ab[:, 0, 0:256])
                        v.tensor_tensor(kd.rearrange("p (h d) -> p h d", h=2),
                                        ab[:, 0, 256:384].rearrange("p (h d) -> p h d", h=2),
                                        C("kdec", 2 * g, 2).unsqueeze(2).to_broadcast([P, 2, 64]), ALU.mult)
                        v.tensor_tensor(sT[:, 0:128], ab[:, 1, 0:128], C("decay", 256 * g, 128), ALU.mult)
                        v.tensor_tensor(sT[:, 128:256], ab[:, 0, 384:512], C("decay", 256 * g + 128, 128), ALU.mult)
                        v.tensor_tensor(qd, pt[:, 0, s], C("qdec", 128 * g, 128),
                                        ALU.mult).then_inc(*sg.on("mid_ready", (u, c)))
                        main(m, 0)
                        dve.wait_ge(*sg.after("stage2", (u, c)))
                        v.tensor_copy(pt[:, 2:4, s], ab[:, :, 0:128])
                        stt(St[:, 0:128], St[:, 0:128], C("cdec", g), ab[:, 0, 256:384], ALU.mult,
                            ALU.add).then_inc(*sg.on("ab_free", (u, c + 1)))
                    main(m, 1)
                both(ms.pop(0))
                d = slice(SEQ, T)
                dve.wait_ge(*sg.after("dec_pe", (u, 0)))
                if u < 2:
                    v.tensor_copy(xtok[0:8, 0:256], ab[0:8, 0, 0:256])
                    xdt = small[:, 32:48].rearrange("p (j b) -> p j b", j=2)
                    v.tensor_tensor(xdt, ab[:, 0, 256:272].rearrange("p (j b) -> p j b", j=2), pt[:, 2:4, d],
                                    ALU.mult).then_inc(*sg.on("dec_ready", (u, 0)))
                    dve.wait_ge(*sg.after("dec_loaded", u))
                    rf = raw[:].rearrange("p a n -> p (a n)")[:, 0:2048].rearrange("p (j b n) -> p j b n", j=2, b=DEC)
                    dve.wait_ge(*sg.after("small_stored", (u, 0)))
                    work = ch[:, 384:384 + 2048].rearrange("p (j b n) -> p j b n", j=2, b=DEC)
                    dve.wait_ge(*sg.after("dec_exp", u))
                    for j in range(2):
                        ed = small[:, 16 + 8 * j:24 + 8 * j].unsqueeze(2).to_broadcast([P, DEC, 128])
                        v.tensor_tensor(rf[:, j], rf[:, j], ed, ALU.mult)
                    dve.wait_ge(*sg.after("dec_pe", (u, 1)))
                    bbc = abf.rearrange("p (b n) -> p b n", b=DEC)
                    for j in range(2):
                        xb = xdt[:, j].unsqueeze(2).to_broadcast([P, DEC, 128])
                        ins = v.tensor_tensor(work[:, j], bbc, xb, ALU.mult)
                    ins.then_inc(*sg.on("dec_ready", (u, 1)))
                    dve.wait_ge(*sg.after("dec_ready", (u, 1)))
                    for j in range(2):
                        ins = v.tensor_tensor(rf[:, j], rf[:, j], work[:, j], ALU.add)
                    ins.then_inc(*sg.on("dec_state_done", u))
                    dve.wait_ge(*sg.after("dec_state_done", u))
                    dve.wait_ge(*sg.after("dec_pe", (u, 2)))
                    for j in range(2):
                        ins = v.tensor_tensor(work[:, j], rf[:, j], bbc, ALU.mult)
                    ins.then_inc(*line.step())
                    dve.wait_ge(*line.last())
                    v.tensor_reduce(small[:, 48:64].rearrange("p (j b) -> p j b", j=2), work, AX_X,
                                    ALU.add).then_inc(*line.step())
                    dve.wait_ge(*line.last())
                    for j in range(2):
                        stt(pt[:, 2 + j, d], pt[:, 2 + j, d], A("ssd_d", 2 * u + j), small[:, 48 + 8 * j:56 + 8 * j],
                                 ALU.mult, ALU.add).then_inc(*line.step())
                        dve.wait_ge(*line.last())
                    dve.wait_ge(*sg.after("gate_act", u))
                    for j in range(2):
                        v.tensor_tensor(pt[:, 2 + j, :], pt[:, 2 + j, :], pt[:, 4 + j, :],
                                        ALU.mult).then_inc(*sg.on("gated", (u, j)))
                    mean_square(pt[:, 4, :], 256, ("norm", u, 0))
                    root_inv(pt[:, 4, :], ("norm", u, 0))
                    for j in range(2):
                        stt(pt[:, 2 + j, :], pt[:, 2 + j, :], A("ssd_g", 2 * u + j), pt[:, 4, :], ALU.mult,
                            ALU.mult).then_inc(*sg.on("y_done", (u, j)))
                else:
                    g = u - 2
                    v.tensor_copy(xtok[0:8, 0:256], ab[0:8, 0, 0:256]).then_inc(*sg.on("dec_ready", (u, 0)))
                    dve.wait_ge(*sg.after("dec_loaded", u))
                    st = raw[:, 0, 0:1024].rearrange("p (b n) -> p b n", b=DEC)
                    work = raw[:, 1, 0:1024].rearrange("p (b n) -> p b n", b=DEC)
                    dve.wait_ge(*sg.after("dec_pe", (u, 1)))
                    v.tensor_tensor(work, abf.rearrange("p (b n) -> p b n", b=DEC),
                                         pt[:, 1, d].unsqueeze(2).to_broadcast([P, DEC, 128]), ALU.mult).then_inc(*line.step())
                    dve.wait_ge(*line.last())
                    stt(raw[:, 0, 0:1024], raw[:, 0, 0:1024], C("gamma", g), raw[:, 1, 0:1024], ALU.mult,
                        ALU.add).then_inc(*sg.on("dec_state_done", u))
                    dve.wait_ge(*sg.after("dec_pe", (u, 2)))
                    v.tensor_copy(pt[:, 2:4, d], ab[:, :, 0:DEC]).then_inc(*sg.on("gated", (u, 1)))
                    dve.wait_ge(*sg.after("small_stored", (u, 1)))
                    for j in range(2):
                        mean_square((T0, T1)[j], RET_DV, ("norm", u, j))
                    dve.wait_ge(*sg.after("gate_act", u))
                    for j in range(2):
                        root_inv((T0, T1)[j], ("norm", u, j))
                        stt(pt[:, 2 + j, :], pt[:, 2 + j, :], A("ret_g", 2 * g + j), (T0, T1)[j], ALU.mult,
                            ALU.mult).then_inc(*line.step())
                        dve.wait_ge(*line.last())
                        v.tensor_tensor(pt[:, 2 + j, :], pt[:, 2 + j, :], pt[:, 4 + j, :],
                                        ALU.mult).then_inc(*sg.on("y_done", (u, j)))
                for j in range(2):
                    split(u, j, pt[:, 2 + j, :])
            for u in range(4, 6):
                ms = list(REST[u])
                for j in range(2):
                    t = 2 * (u - 4) + j
                    dve.wait_ge(*sg.after(f"raw_loaded{j}", (u, j)))
                    v.memset(raw[:, j, 0:3], 0.0).then_inc(*line.step())
                    dve.wait_ge(*line.last())
                    ins = conv(u, j, pt[:, j, :], raw[:, j, :], lambda k: A("lru_w", 4 * t + k),
                               lambda k: A("lru_prev", 24 * t + 8 * k, 8), LRU_W)
                    ins.then_inc(*sg.on("conv_done", (u, j)))
                both(ms[0])
                for j in range(2):
                    dve.wait_ge(*sg.after("sig", (u, j, 2)))
                    v.tensor_tensor(pt[:, 4 + j, :], pt[:, 4 + j, :], pt[:, j, :], ALU.mult).then_inc(*line.step())
                    dve.wait_ge(*line.last())
                for j in range(2):
                    t = 2 * (u - 4) + j
                    dve.wait_ge(*sg.after("a_done", (u, j)))
                    v.tensor_tensor(pt[:, j, :], pt[:, 2 + j, :], pt[:, 2 + j, :], ALU.mult).then_inc(*line.step())
                    dve.wait_ge(*line.last())
                    stt((T0, T1)[j], pt[:, j, :], 1.0, (T0, T1)[j], ALU.add,
                        ALU.mult).then_inc(*sg.on("e_done", (u, j)))
                for j in range(2):
                    t = 2 * (u - 4) + j
                    dve.wait_ge(*sg.after("lru_root", (u, j)))
                    v.tensor_tensor(pt[:, 4 + j, :], pt[:, 4 + j, :], (T0, T1)[j], ALU.mult).then_inc(*line.step())
                    dve.wait_ge(*line.last())
                    d = slice(SEQ, T)
                    v.tensor_tensor_scan(pt[:, j, 0:SEQ], pt[:, 2 + j, 0:SEQ], pt[:, 4 + j, 0:SEQ], 0.0,
                                              ALU.mult, ALU.add).then_inc(*line.step())
                    dve.wait_ge(*line.last())
                    v.tensor_tensor(pt[:, j, d], pt[:, 2 + j, d], A("lru_h0", 8 * t, 8),
                                    ALU.mult).then_inc(*line.step())
                    dve.wait_ge(*line.last())
                    v.tensor_tensor(pt[:, j, d], pt[:, j, d], pt[:, 4 + j, d],
                                    ALU.add).then_inc(*sg.on("h_done", (u, j)))
                for j in range(2):
                    dve.wait_ge(*sg.after("h_done", (u, j)))
                    dve.wait_ge(*sg.after("gelu", (u, j)))
                    v.tensor_tensor(pt[:, 4 + j, :], pt[:, j, :], raw[:, j, 0:T],
                                    ALU.mult).then_inc(*sg.on("y_done", (u, j)))
                both(ms[1])
                for j in range(2):
                    split(u, j, pt[:, 4 + j, :])
            for m in REST[6]:
                both(m)
            refresh(KD - 1, layer * 2 + 1, "ffn")
            mean_square(rstd[:], D_MODEL, "norm2")
            root_inv(rstd[:], "norm2")
            for j in range(2):
                v.memset(raw[:, j, 0:2], 0.0).then_inc(*line.step())
                dve.wait_ge(*line.last())

            def up_part(blk, tag, r0, base):
                for j in range(2):
                    r = r0 + j
                    dve.wait_ge(sg.sem("m_ready"), layer * RUSES + base + (r + 1))
                    if tag == "loop":
                        dve.wait_ge(sg.sem(f"ffn_stored{j}"), layer * (16 * FB) + (b + 1) * 16)
                    v.tensor_tensor(g3(raw[:, j, 2:T + 2]), ring[:, r % 2, :, 0:TG], g3(rstd[:]),
                                    ALU.mult).then_inc(*sg.on("m_free", ("ffn", r)))
                for j in range(2):
                    dve.wait_ge(*sg.after("ffn_tap", (tag, j)))
                    for k in range(2):
                        w = pick(par, COL["ffn_w"], blk, 6, 3 * j + k)
                        pv = pick(par, COL["ffn_prev"], blk, 32, 16 * j + 8 * k, 8)
                        stt(pt[:, j, 0:SEQ], raw[:, j, k:k + SEQ], w, pt[:, j, 0:SEQ], ALU.mult,
                            ALU.add).then_inc(*line.step())
                        dve.wait_ge(*line.last())
                        ins = stt(pt[:, j, SEQ:T], pv, w, pt[:, j, SEQ:T], ALU.mult, ALU.add)
                        if k == 0:
                            ins.then_inc(*line.step())
                            dve.wait_ge(*line.last())
                    ins.then_inc(*sg.on("ffn_conv", (tag, j)))
                for j in range(2):
                    r = r0 + 2 + j
                    dve.wait_ge(sg.sem("m_ready"), layer * RUSES + base + (r + 1))
                    v.tensor_tensor(g3(pt[:, 2 + j, :]), ring[:, r % 2, :, 0:TG], g3(rstd[:]),
                                    ALU.mult).then_inc(*sg.on("m_free", ("ffn", r)))

            def y_part(tag, r, base):
                dve.wait_ge(*freed(layer, r, base))
                for j in range(2):
                    dve.wait_ge(*sg.after("ffn_gelu", (tag, j)))
                    v.tensor_tensor(pt[:, 2 + j, :], pt[:, 2 + j, :], pt[:, j, :],
                                    ALU.mult).then_inc(*sg.on("ffn_y", (tag, j)))
                for j in range(2):
                    dve.wait_ge(*sg.after("ffn_hi", (tag, j)))
                    ins = v.tensor_tensor(y_lo[:, j, :], pt[:, 2 + j, :], y_hi[:, j, :].bitcast(F32), ALU.subtract)
                ins.then_inc(*sg.on("ffn_split", tag))

            up_part(0, "first", R0, 0)
            y_part("first", R0 + 3, 0)
            with dve.Fori(0, FB - 1) as b, sg.loop("ffn", FB - 1, b):
                up_part(b + 1, "loop", R0 + 4, b * 12)
                for mo in range(KD):
                    r = R0 + 8 + mo
                    dve.wait_ge(sg.sem("m_ready"), layer * RUSES + b * 12 + (r + 1))
                    v.tensor_tensor(g3(x[:, mo, :]), ring[:, r % 2, :, 0:TG], g3(x[:, mo, :]),
                                    ALU.add).then_inc(*sg.on("m_free", ("ffn", r)))
                y_part("loop", R0 + 7, b * 12)
            dve.wait_ge(*sg.after("ffn_split", "loop"))
            v.nop().then_inc(*sg.on("par_free"))
            for mo in range(KD):
                r = R0 + 4 + mo
                dve.wait_ge(sg.sem("m_ready"), layer * RUSES + 12 * (FB - 1) + (r + 1))
                v.tensor_tensor(g3(x[:, mo, :]), ring[:, r % 2, :, 0:TG], g3(x[:, mo, :]),
                                ALU.add).then_inc(*sg.on("m_free", ("last", r)))
                if mo >= 1:
                    refresh(mo - 1, layer * 2 + 2, "next")
            refresh(KD - 1, layer * 2 + 2, "next")
        dve.wait_ge(*sg.after("last_sum"))
        v.tensor_scalar(g3(rstd[:]), ring[:, 0, :, 0:TG], 1.0 / D_MODEL, EPS, ALU.mult,
                        ALU.add).then_inc(*sg.on("last_ms"))
        dve.wait_ge(*sg.after("last_root"))
        v.reciprocal(rstd[:], rstd[:]).then_inc(*sg.on("last_rstd"))
        dve.wait_ge(*sg.after("last_rstd"))
        for m in range(KD):
            if m >= 2:
                dve.wait_ge(*sg.after(f"y_stored{m % 2}", m - 2))
            stt(ev[:, m % 2, :], x[:, m, :], gains[:, 2 * DEPTH * KD + m:2 * DEPTH * KD + m + 1], rstd[:],
                     ALU.mult, ALU.mult).then_inc(*sg.on("y_ready", m))
    return sg


def constants():
    f8 = np.float64
    log_g = np.log1p(-np.exp2(-5.0 - np.arange(RET_H, dtype=f8)))
    i = np.arange(CHUNK, dtype=f8)
    con = np.zeros((P, NCON), np.float32)

    def put(name, a):
        a = np.asarray(a, np.float32)
        con[:a.shape[0], CON[name]:CON[name] + a.shape[1]] = a
    put("ident", np.eye(P))
    causal = (i[:, None] <= i[None, :])
    put("causal", causal)
    for h in range(RET_H):
        con[:, CON["decay"] + h * 128:CON["decay"] + (h + 1) * 128] = \
            np.where(causal, np.exp(np.maximum(i[None, :] - i[:, None], 0) * log_g[h]), 0)
        con[:, CON["kdec"] + h] = np.exp((CHUNK - 1.0 - i) * log_g[h])
        rows = slice(64 * (h % 2), 64 * (h % 2) + 64)
        c = CON["qdec"] + 128 * (h // 2)
        con[rows, c:c + 128] = np.exp((i + 1.0) * log_g[h])[None, :]
        con[rows, CON["cdec"] + h // 2] = np.exp(CHUNK * log_g[h])
        con[rows, CON["gamma"] + h // 2] = np.exp(log_g[h])
    for b in range(8):
        con[b, CON["sel"] + b * 128:CON["sel"] + (b + 1) * 128] = 1
    half = RET_DK // 2
    freqs = np.float32(10000.0) ** (-np.arange(half, dtype=np.float32) / np.float32(half))
    pos = np.concatenate([np.arange(SEQ), np.full(DEC, PAST_LEN)]).astype(np.float32)
    ang = (freqs[:, None] * pos[None, :]).astype(np.float32).astype(f8)
    cos = np.tile(np.cos(ang), (4, 1)).astype(np.float32)
    sin = np.tile(np.concatenate([-np.sin(ang), np.sin(ang)]), (2, 1)).astype(np.float32)
    return con, cos, sin


def feature_cols():
    lx, lg, rq, rk, rv, rgt, z, xbc, dt = np.cumsum([0, 512, 512, 256, 256, 512, 512, 512, 1024])
    xs, bm, cm = xbc, xbc + 512, xbc + 768
    starts = []
    for g in range(2):
        starts += [bm + 128 * g, cm + 128 * g, xs + 256 * g, xs + 256 * g + 128, z + 256 * g, z + 256 * g + 128]
    for g in range(2):
        starts += [rq + 128 * g, rk + 128 * g, rv + 256 * g, rv + 256 * g + 128, rgt + 256 * g, rgt + 256 * g + 128]
    for p in range(2):
        starts += [lx + 256 * p, lx + 256 * p + 128, lg + 256 * p, lg + 256 * p + 128]
    return starts, int(dt)


def lay_out(i):
    f = np.float32
    L = DEPTH
    d = {}
    x = np.concatenate([i["x_prompt"][0], i["x_sample"][:, 0]], axis=0)
    d["x"] = x.T.reshape(KD, P, T)
    starts, dt0 = feature_cols()
    w = np.zeros((L, SLOTS, P, 1024), f)

    def up_slot(wm, c0):
        return wm[:, c0:c0 + P].reshape(KD, P, P).transpose(1, 0, 2).reshape(P, 1024)

    def down_slot(wm, rows, half):
        a = wm[rows[0]:rows[0] + P], wm[rows[1]:rows[1] + P]
        a = np.stack([t[:, 512 * half:512 * half + 512].reshape(P, 4, P) for t in a], axis=2)
        return a.reshape(P, 1024)
    mix0 = [1024, 1280, 512, 768, 0, 256]
    for l in range(L):
        for s, m in enumerate(ORDER):
            if m[0] == "in":
                w[l, s] = up_slot(i["w_in"][l], starts[m[1]])
            else:
                r = mix0[m[1]]
                w[l, s] = down_slot(i["w_out"][l], (r, r + P), m[2])
        s = len(ORDER)
        up, down = i["ffn_w_up"][l], i["ffn_w_down"][l]

        def ups(b):
            return [up_slot(up, c) for c in (256 * b, 256 * b + 128, D_FF + 256 * b, D_FF + 256 * b + 128)]

        def downs(b):
            return [down_slot(down, (256 * b, 256 * b + 128), h) for h in range(2)]
        seq = ups(0)
        for b in range(FB - 1):
            seq += ups(b + 1) + downs(b)
        seq += downs(FB - 1)
        w[l, s:] = np.stack(seq)
    d["w"] = w.reshape(L * SLOTS, P, 1024)
    par = np.zeros((L, P, NPAR), f)

    def put(l, name, a):
        par[l, :a.shape[0], COL[name]:COL[name] + a.shape[1]] = a

    def tiles(v):
        return v.reshape(-1, P).T

    def taps(wc, order):
        return np.concatenate([wc[:, c:c + P].T for c in order], axis=1)

    def past(st, order):
        return np.concatenate([st[:, :, c:c + P].transpose(2, 1, 0).reshape(P, -1) for c in order], axis=1)
    so = []
    for g in range(2):
        so += [512 + 128 * g, 768 + 128 * g, 256 * g, 256 * g + 128]
    lo = [0, 128, 256, 384]
    fo = [128 * n for n in range(FT)]
    for l in range(L):
        put(l, "lru_w", taps(i["lru_conv_w"][l], lo))
        put(l, "lru_b", tiles(i["lru_conv_b"][l]))
        put(l, "br", tiles(i["lru_br"][l]))
        put(l, "bi", tiles(i["lru_bi"][l]))
        put(l, "lam", tiles(i["lru_lambda"][l]))
        put(l, "ret_g", i["ret_norm_g"][l].T)
        put(l, "ssd_w", taps(i["ssd_conv_w"][l], so))
        put(l, "ssd_b", np.stack([i["ssd_conv_b"][l][c:c + P] for c in so], axis=1))
        put(l, "ssd_d", tiles(np.repeat(i["ssd_d"][l], 64)))
        put(l, "ssd_g", tiles(i["ssd_norm_g"][l]))
        put(l, "dt_bias", np.broadcast_to(i["ssd_dt_bias"][l], (P, 8)))
        put(l, "a_log", np.broadcast_to(i["ssd_a_log"][l], (P, 8)))
        put(l, "ffn_w", taps(i["ffn_conv_w"][l], fo))
        put(l, "ffn_b", tiles(i["ffn_conv_b"][l]))
        put(l, "lru_h0", np.concatenate([i["state_lru_h"][l][:, c:c + P].T for c in lo], axis=1))
        put(l, "lru_prev", past(i["state_lru_conv"][l], lo))
        put(l, "ssd_prev", past(i["state_ssd_conv"][l], so))
        put(l, "ffn_prev", past(i["state_ffn_conv"][l], fo))
        put(l, "wdt", i["w_in"][l][:, dt0:dt0 + 8].reshape(KD, P, 8).transpose(1, 0, 2).reshape(P, 64))
    d["par"] = par
    g = []
    for l in range(L):
        g += [tiles(i["norm_mix_g"][l]), tiles(i["norm_ffn_g"][l])]
    d["gains"] = np.concatenate(g + [tiles(i["norm_final_g"])], axis=1)
    gw = np.zeros((L, 2, P, 4, P), f)
    for l in range(L):
        for t in range(4):
            for n, name in enumerate(("lru_wr", "lru_wi")):
                for q in range(2):
                    s = slice(64 * q, 64 * q + 64)
                    gw[l, t // 2, s, 2 * (t % 2) + n, s] = i[name][l, 2 * t + q]
    d["gate_w"] = gw
    d["ret_state"] = i["state_ret"].reshape(L, 8, 2, 2, 64, 128).transpose(0, 2, 3, 4, 1, 5).reshape(L, 2, P, 1024)
    d["ssd_state"] = i["state_ssd"].reshape(L, 8, 2, 2, 2, 64, 128).transpose(0, 2, 4, 5, 3, 1, 6).reshape(L, 2, P, 2, 1024)
    d["i_lru_old"] = i["state_lru_conv"][:, :, 1:]
    d["i_ssd_old"] = i["state_ssd_conv"][:, :, 1:]
    d["i_ffn_old"] = i["state_ffn_conv"][:, :, 1:]
    d["con"], d["cos"], d["sin"] = constants()
    return {k: np.ascontiguousarray(a, dtype=f) for k, a in d.items()}


OUTS = {
    "y": (KD, P, T),
    "o_lru_old": (DEPTH, 8, 2, 512), "o_ssd_old": (DEPTH, 8, 2, 1024), "o_ffn_old": (DEPTH, 8, 1, D_FF),
    "o_lru_new": (DEPTH, 4, P, 11), "o_ssd_new": (DEPTH, 8, P, 11), "o_ffn_new": (DEPTH, FT, P, 10),
    "o_lru_h": (DEPTH, 4, P, 9),
    "o_ret_p": (DEPTH, 2, P, 128), "o_ret_s": (DEPTH, 2, P, 1024),
    "o_ssd_p": (DEPTH, 2, P, 256), "o_ssd_s": (DEPTH, 2, P, 2, 1024),
}


def give_back(r):
    L = DEPTH
    y = r["y"].reshape(D_MODEL, T).T
    y_p, y_s = y[None, :SEQ], y[SEQ:, None]

    def conv_state(new, old, order, n):
        width = new.shape[1] * P
        at = np.argsort(order)
        a = new[:, at].reshape(L, width, -1)
        p = a[:, :, :n].transpose(0, 2, 1)[:, None]
        s = np.concatenate([old, a[:, :, n:].transpose(0, 2, 1)[:, :, None]], axis=2)
        return p, s
    so = []
    for g in range(2):
        so += [512 + 128 * g, 768 + 128 * g, 256 * g, 256 * g + 128]
    lc_p, lc_s = conv_state(r["o_lru_new"], r["o_lru_old"], range(4), 3)
    sc_p, sc_s = conv_state(r["o_ssd_new"], r["o_ssd_old"], so, 3)
    fc_p, fc_s = conv_state(r["o_ffn_new"], r["o_ffn_old"], range(FT), 2)
    h = r["o_lru_h"].reshape(L, 512, 9)
    h_p, h_s = h[:, :, 0][:, None], h[:, :, 1:].transpose(0, 2, 1)
    ret_p = r["o_ret_p"].reshape(L, 1, 4, 64, 128)
    ret_s = r["o_ret_s"].reshape(L, 2, 2, 64, 8, 128).transpose(0, 4, 1, 2, 3, 5).reshape(L, 8, 4, 64, 128)
    ssd_p = r["o_ssd_p"].reshape(L, 2, P, 4, 64).transpose(0, 1, 3, 4, 2).reshape(L, 1, 8, 64, 128)
    ssd_s = r["o_ssd_s"].reshape(L, 2, 2, 64, 2, 8, 128).transpose(0, 5, 1, 4, 2, 3, 6).reshape(L, 8, 8, 64, 128)
    out = (y_p, y_s, lc_p, lc_s, h_p, h_s, ret_p, ret_s, sc_p, sc_s, ssd_p, ssd_s, fc_p, fc_s)
    return tuple(np.ascontiguousarray(a) for a in out)


def program(nc, arrays, before):
    io = {k: nc.dram_tensor(k, a.shape, F32, kind="ExternalInput").ap() for k, a in arrays.items()}
    for k, shape in OUTS.items():
        io[k] = nc.dram_tensor(k, shape, F32, kind="ExternalOutput").ap()
    io["proj"] = nc.dram_tensor("proj", (IN_TILES, P, T), F32, kind="Internal").ap()
    with ExitStack() as ctx:
        return build(nc, io, ctx, before)


def kernel(**inputs):
    import concourse.bacc as bacc
    from concourse.bass_utils import run_bass_kernel_spmd

    arrays = lay_out({k: np.asarray(a) for k, a in inputs.items()})
    before = program(bacc.Bacc("TRN2", target_bir_lowering=False, num_devices=1), arrays, None)
    nc = bacc.Bacc("TRN2", target_bir_lowering=False, num_devices=1)
    program(nc, arrays, before)
    r = run_bass_kernel_spmd(nc, [arrays], core_ids=[0]).results[0]
    return give_back({k: r[k] for k in OUTS})
```

```python
from contextlib import ExitStack

import numpy as np

import concourse.bass as bass
from concourse import mybir

ALU = mybir.AluOpType
ACT = mybir.ActivationFunctionType
F32 = mybir.dt.float32
F32R = mybir.dt.float32r
AX_X = mybir.AxisListType.X

P = 128
D_MODEL, SEQ, DEPTH, DEC = 1024, 1024, 2, 8
PAST_LEN = 8192
T = SEQ + DEC
NG = 3
TG = T // NG
KD = D_MODEL // P
CHUNK = 128
NCH = SEQ // CHUNK
D_FF = 2816
FT = D_FF // P
FB = FT // 2
IN_TILES = 32
LRU_W, FFN_W = 4, 3
RET_H, RET_DK, RET_DV = 4, 64, 128
SSD_H = 8
EPS = 1e-6
SLOTS = IN_TILES + 12 + 6 * FB

_widths = [("lru_w", 16), ("lru_b", 4), ("br", 4), ("bi", 4), ("lam", 4), ("ret_g", 4),
           ("ssd_w", 32), ("ssd_b", 8), ("ssd_d", 4), ("ssd_g", 4), ("dt_bias", 8), ("a_log", 8),
           ("ffn_w", 66), ("ffn_b", 22), ("lru_h0", 32), ("lru_prev", 96), ("ssd_prev", 192),
           ("ffn_prev", 352), ("wdt", 64)]
COL, NPAR = {}, 0
for _n, _w in _widths:
    COL[_n] = NPAR
    NPAR += _w

_consts = [("ident", 128), ("causal", 128), ("decay", 512), ("sel", 1024), ("qdec", 256),
           ("kdec", 4), ("cdec", 2), ("gamma", 2)]
CON, NCON = {}, 0
for _n, _w in _consts:
    CON[_n] = NCON
    NCON += _w

UNITS = ["S0", "S1", "R0", "R1", "L0", "L1"]
TILE0 = {"S0": 0, "S1": 6, "R0": 12, "R1": 18, "L0": 24, "L1": 28}


def ins(a, b):
    return [("in", i) for i in range(a, b)]


def out(u):
    return [("out", u, 0), ("out", u, 1)]


FIRST = ins(0, 6)
DURING = [ins(6, 14), out(0) + ins(14, 20), out(1) + ins(20, 25), out(2) + ins(25, 29), out(3) + ins(29, 32), out(4)]
LAST = out(5)
ORDER = FIRST + [m for ms in DURING for m in ms] + LAST
assert len(ORDER) == 44
CHUNKS_A = [f"a{c}" for c in range(NCH)]
HALVES = [
    {"pre": 4, "a": 7, "d0": 1, "d1": 1, "d2": 1, "fin": 2},
    {"pre": 4, "a": 8, "d0": 1, "d1": 0, "d2": 1, "fin": 2},
    {"pre": 4, "a": 5, "d0": 1, "d1": 0, "d2": 0, "fin": 4},
    {"pre": 4, "a": 5, "d0": 1, "d1": 0, "d2": 0, "fin": 2},
    {"pre": 4, "g": 2, "fin": 4},
    {"pre": 2, "g": 0, "fin": 2},
]


def schedule():
    plan = []
    for ms, counts in zip(DURING, HALVES):
        halves = [(m, k) for m in ms for k in range(2)]
        assert sum(counts.values()) == len(halves) and counts["fin"] % 2 == 0
        at = {}
        for point, n in counts.items():
            if point == "a":
                for c in range(NCH):
                    k = n * (c + 1) // NCH - n * c // NCH
                    at[f"a{c}"], halves = halves[:k], halves[k:]
            else:
                at[point], halves = halves[:n], halves[n:]
        plan.append(at)
    return plan


PLAN = schedule()


def ring_uses():
    at = {"norm": 0, FIRST[0]: 1, "dt": 2}
    n = 3

    def product(m, half, n):
        if m[0] == "in":
            if half == 0:
                at[m] = n
                return n + 1
            return n
        for i in range(2):
            at[m + (2 * half + i,)] = n + i
        return n + 2
    for m in FIRST[1:]:
        n = product(m, 0, n)
    for u, points in enumerate(PLAN):
        for point, halves in points.items():
            if point == "fin" and u < 4:
                for i in range(1 if u < 2 else 2):
                    at["norm", u, i] = n
                    n += 1
            for m, half in halves:
                n = product(m, half, n)
    for m in LAST:
        for half in range(2):
            n = product(m, half, n)
    at["norm2"] = n
    return at, n + 1


RING, R0 = ring_uses()
RUSES = R0 + 12 * FB
FREE = 1


class Signals:

    def __init__(self, nc, ctx, before):
        self.nc, self.ctx, self.before = nc, ctx, before
        self.sems, self.count, self.at, self.delta = {}, {}, {}, {}
        self.loops, self.turns = [], {}

    def sem(self, kind):
        if kind not in self.sems:
            self.sems[kind] = self.ctx.enter_context(self.nc.semaphore(kind))
        return self.sems[kind]

    def on(self, kind, key=None, n=1):
        self.count[kind] = self.count.get(kind, 0) + n
        self.at[kind, key] = (self.count[kind], [x for x, _ in self.loops])
        return self.sem(kind), n

    def loop(self, name, turns, var):
        return _Loop(self, name, turns, var)

    def value(self, kind, key, last=False):
        src = self.before or self
        if (kind, key) not in src.at:
            assert self.before is None, (kind, key)
            return 1
        first, loops = src.at[kind, key]
        now = dict(self.loops)
        v = first
        for x in loops:
            step = src.delta.get((x, kind), 0)
            v = v + now[x] * step if x in now else v + (src.turns[x] - 1) * step
        return v

    def after(self, kind, key=None):
        return self.sem(kind), self.value(kind, key)


class Line:

    def __init__(self, sg, kind):
        self.sg, self.kind, self.n = sg, kind, 0

    def step(self):
        self.n += 1
        return self.sg.on(self.kind, self.n)

    def last(self):
        return self.sg.after(self.kind, self.n)


def pick(tile, base, blk, stride, off, n=1):
    if isinstance(blk, int):
        at = base + blk * stride + off
        return tile[:, at:at + n]
    return tile[:, bass.ds(blk * stride + (base + off), n)]


class _Loop:
    def __init__(self, s, name, turns, var):
        self.s, self.name, self.turns, self.var = s, name, turns, var

    def __enter__(self):
        self.s.loops.append((self.name, self.var))
        self.start = dict(self.s.count)
        return self.var

    def __exit__(self, *a):
        s = self.s
        s.loops.pop()
        s.turns[self.name] = self.turns
        for k, v in s.count.items():
            d = v - self.start.get(k, 0)
            if d:
                s.delta[self.name, k] = d
                s.count[k] = v + d * (self.turns - 1)


def build(nc, io, ctx, before):
    sg = Signals(nc, ctx, before)

    def sb(name, shape, dt=F32):
        return ctx.enter_context(nc.sbuf_tensor("sb_" + name, shape, dt))

    x = sb("x", [P, KD, T])
    h_hi = sb("h_hi", [P, KD, T], F32R)
    h_lo = sb("h_lo", [P, KD, T], F32R)
    w_raw = sb("w_raw", [P, 2, 1024])
    w_hi = sb("w_hi", [P, 2, 1024], F32R)
    w_lo = sb("w_lo", [P, 2, 1024], F32R)
    y_hi = sb("y_hi", [P, 2, T], F32R)
    y_lo = sb("y_lo", [P, 2, T], F32R)
    rstd = sb("rstd", [P, T])
    pt = sb("pt", [P, 6, T])
    raw = sb("raw", [P, 2, T + 3])
    ev = sb("ev", [P, 2, T])
    ch = sb("ch", [P, 2568])
    par = sb("par", [P, NPAR])
    gains = sb("gains", [P, (2 * DEPTH + 1) * KD])
    con = sb("con", [P, NCON])
    tok = sb("tok", [P, 5, 72])
    ones = sb("ones", [P, P])
    gate_w = sb("gate_w", [P, 4, P])
    wdt = sb("wdt", [P, 64])
    small = sb("small", [P, 64])
    rms = sb("rms", [P, 2, NCH + 1])
    rgc = sb("rgc", [P, 4, 6])
    ring = ctx.enter_context(nc.psum_tensor("ring", [P, 2, NG, 512], F32))
    ab = ctx.enter_context(nc.psum_tensor("ab", [P, 2, 512], F32))
    abf = ab[:].rearrange("p a n -> p (a n)")

    def C(name, i=0, n=1):
        return con[:, CON[name] + i:CON[name] + i + n]

    def A(name, i=0, n=1):
        return par[:, COL[name] + i:COL[name] + i + n]

    ident = C("ident", 0, 128)
    T0, T1 = ch[:, 0:T], ch[:, T:2 * T]
    Btok, xtok, xw, cbm = ch[:, 0:128], ch[:, 128:384], ch[:, 384:640], ch[:, 640:768]
    seg, Ec, Ce, St = ch[:, 768:1284], ch[:, 1284:1796], ch[:, 1796:2308], ch[:, 2308:2564]
    kd, qd, sT, vtok = Btok, cbm, xw, xtok

    def g3(ap):
        return ap.rearrange("p (g n) -> p g n", g=NG)

    def cols(c):
        return slice(c * CHUNK, (c + 1) * CHUNK)

    def freed(layer, r, base=0):
        return sg.sem("m_free"), layer * RUSES + base + (r + 1 + FREE)

    block = ctx.enter_context(nc.Block())

    class Ring:
        def __init__(self):
            self.r = 0

        def next(self):
            self.r += 1
            return self.r - 1

    @block.sync
    def _(sp):
        def step():
            sp.sem_inc(sg.sem("sync_steps"), 1)

        sp.dma_start(con[:], io["con"]).then_inc(*sg.on("const_loaded", None, 16))
        sp.dma_start(gains[:], io["gains"]).then_inc(*sg.on("gains_loaded", None, 16))
        for m in range(KD):
            sp.dma_start(x[:, m, :], io["x"][m]).then_inc(*sg.on(f"x_loaded{m}", None, 16))
        for name in ("lru", "ssd", "ffn"):
            sp.dma_start(io[f"o_{name}_old"], io[f"i_{name}_old"]).then_inc(*sg.on("old_rows", None, 16))

        def weights(s, first=False):
            sp.wait_ge(sg.sem("w_split_done"), layer * SLOTS + (max(s - 1, 0) + FREE))
            step()
            sp.dma_start(w_raw[:, s % 2, :], io["w"][layer * SLOTS + s]).then_inc(*sg.on(f"w_raw{s % 2}", s, 16))

        with sp.Fori(0, DEPTH) as layer, sg.loop("layer", DEPTH, layer):
            sp.wait_ge(sg.sem("par_free"), layer + FREE)
            step()
            sp.dma_start(par[:], io["par"][layer]).then_inc(*sg.on("par_loaded", None, 16))
            weights(0)
            weights(1)
            fill = [2]

            def more(upto):
                while fill[0] < min(upto, SLOTS):
                    weights(fill[0])
                    fill[0] += 1

            def spill(i):
                sp.wait_ge(*freed(layer, RING["in", i]))
                step()
                sp.dma_start(io["proj"][i], ev[:, i % 2, :]).then_inc(*sg.on(f"ev_stored{i % 2}", i, 16))

            def stored(i):
                sp.wait_ge(*sg.after(f"ev_stored{i % 2}", i))
                step()

            slot = [0]

            def main(m):
                more(slot[0] + 3)
                if m[0] == "in":
                    spill(m[1])
                slot[0] += 1
                more(slot[0] + 3)

            def ended(halves):
                for m, half in halves:
                    if half == 1:
                        main(m)

            def load_conv(u, j, tile):
                stored(tile)
                if j >= 2:
                    sp.wait_ge(*sg.after("conv_done", (u, j - 2)))
                    step()
                sp.dma_start(raw[:, j % 2, 3:T + 3],
                             io["proj"][tile]).then_inc(*sg.on("raw_loaded" + str(j % 2), (u, j), 16))

            def prep_early(u):
                t0 = TILE0[UNITS[u]]
                if u > 0:
                    sp.wait_ge(*sg.after("small_stored", (u - 1, 1)))
                    step()
                if 0 < u < 5:
                    sp.wait_ge(*sg.after("sq_turned", (u - 1, 0 if u < 3 else 1)))
                    step()
                elif u == 5:
                    sp.wait_ge(*sg.after("y_done", (4, 1)))
                    step()
                if u in (2, 3):
                    sp.dma_start(T0, io["cos"]).then_inc(*sg.on("rope_loaded", (u, 0), 16))
                    sp.dma_start(T1, io["sin"]).then_inc(*sg.on("rope_loaded", (u, 1), 16))
                    for j in range(2):
                        stored(t0 + j)
                        sp.dma_start(pt[:, j, :], io["proj"][t0 + j]).then_inc(*sg.on("qk_loaded", (u, j), 16))
                        for q in range(4):
                            src = io["proj"][t0 + j, 32 * (q ^ 1):32 * (q ^ 1) + 32, :]
                            sp.dma_start(raw[32 * q:32 * q + 32, j, 0:T], src).then_inc(*sg.on("qk_loaded", (u, j, q), 16))
                else:
                    for j in range(2):
                        load_conv(u, j, t0 + j)

            def prep(u):
                t0 = TILE0[UNITS[u]]
                if u > 0:
                    sp.wait_ge(*sg.after("y_split", u - 1))
                    step()
                if u < 2:
                    for j in (2, 3):
                        load_conv(u, j, t0 + j)
                    for j in (4, 5):
                        stored(t0 + j)
                        sp.dma_start(pt[:, j, :], io["proj"][t0 + j]).then_inc(*sg.on("gate_loaded", (u, j), 16))
                elif u < 4:
                    for j in range(2, 6):
                        stored(t0 + j)
                        sp.dma_start(pt[:, j, :], io["proj"][t0 + j]).then_inc(*sg.on("vg_loaded", (u, j), 16))
                else:
                    sp.dma_start(gate_w[:], io["gate_w"][layer, u - 4]).then_inc(*sg.on("gate_w_loaded", u, 16))
                    for j in (2, 3):
                        stored(t0 + j)
                        sp.wait_ge(*sg.after("conv_done", (u, j - 2)))
                        step()
                        sp.dma_start(raw[:, j - 2, 0:T], io["proj"][t0 + j]).then_inc(*sg.on("gate_loaded", (u, j), 16))

            def load_states(u):
                if u < 2:
                    sp.wait_ge(*sg.after("conv_done", (u, 3)))
                    step()
                    sp.wait_ge(*sg.after("conv_done", (u, 2)))
                    step()
                    rf = raw[:].rearrange("p a n -> p (a n)")[:, 0:2048].rearrange("p (a n) -> p a n", a=2)
                    sp.dma_start(rf, io["ssd_state"][layer, u]).then_inc(*sg.on("dec_loaded", u, 16))
                elif u < 4:
                    sp.wait_ge(*sg.after("rope_done", u))
                    step()
                    sp.dma_start(raw[:, 0, 0:1024],
                                 io["ret_state"][layer, u - 2]).then_inc(*sg.on("dec_loaded", u, 16))

            def store_prompt_state(u):
                sp.wait_ge(*sg.after("ab_free", (u, NCH)))
                step()
                if u < 2:
                    sp.dma_start(io["o_ssd_p"][layer, u], St).then_inc(*sg.on("small_stored", (u, 0), 16))
                else:
                    sp.dma_start(io["o_ret_p"][layer, u - 2], St[:, 0:128]).then_inc(*sg.on("small_stored", (u, 0), 16))

            def store_sample_states(u):
                sp.wait_ge(*sg.after("dec_state_done", u))
                step()
                if u < 2:
                    rf = raw[:].rearrange("p a n -> p (a n)")[:, 0:2048].rearrange("p (a n) -> p a n", a=2)
                    sp.dma_start(io["o_ssd_s"][layer, u], rf).then_inc(*sg.on("small_stored", (u, 1), 16))
                else:
                    sp.dma_start(io["o_ret_s"][layer, u - 2], raw[:, 0, 0:1024]).then_inc(*sg.on("small_stored", (u, 1), 16))

            def store_h(u):
                for j in range(2):
                    sp.wait_ge(*sg.after("h_done", (u, j)))
                    step()
                    sp.dma_start(io["o_lru_h"][layer, 2 * (u - 4) + j],
                                 pt[:, j, SEQ - 1:T]).then_inc(*sg.on("small_stored", (u, j), 16))

            for m in FIRST:
                main(m)
            prep_early(0)
            for u in range(6):
                prep(u)
                ended(PLAN[u]["pre"])
                if u < 4:
                    ended(PLAN[u]["a0"])
                    ended(PLAN[u]["a1"])
                    load_states(u)
                    for c in range(2, NCH):
                        ended(PLAN[u][f"a{c}"])
                    store_prompt_state(u)
                    ended(PLAN[u]["d0"])
                    ended(PLAN[u]["d1"])
                    store_sample_states(u)
                    ended(PLAN[u]["d2"])
                    prep_early(u + 1)
                    ended(PLAN[u]["fin"])
                else:
                    ended(PLAN[u]["g"])
                    store_h(u)
                    if u == 4:
                        ended(PLAN[u]["fin"][:2])
                        prep_early(5)
                        ended(PLAN[u]["fin"][2:])
                    else:
                        ended(PLAN[u]["fin"])
            for m in LAST:
                main(m)
            for i in range(IN_TILES):
                if i >= IN_TILES - 2:
                    stored(i)
            for j in range(2):
                sp.dma_start(io["o_ssd_new"][layer, 4 * j:4 * j + 4],
                             io["proj"][6 * j:6 * j + 4, :, SEQ - 3:T]).then_inc(*sg.on("rows_stored", j, 16))
                sp.dma_start(io["o_lru_new"][layer, 2 * j:2 * j + 2],
                             io["proj"][24 + 4 * j:26 + 4 * j, :, SEQ - 3:T]).then_inc(*sg.on("rows_stored", 2 + j, 16))

            s0 = 44
            for s in range(4):
                more(s0 + s + 3)

            sp.wait_ge(*sg.after("rows_stored", 3))
            step()
            for j in range(2):
                sp.wait_ge(*freed(layer, R0 + j))
                step()
                sp.dma_start(io["o_ffn_new"][layer, j],
                             raw[:, j, SEQ:T + 2]).then_inc(*sg.on(f"ffn_stored{j}", "first", 16))
            assert fill[0] == s0 + 6
            with sp.Fori(0, FB - 1) as b, sg.loop("ffn", FB - 1, b):
                for s in range(6):
                    sp.wait_ge(sg.sem("w_split_done"), layer * SLOTS + b * 6 + (s0 + 5 + s + FREE))
                    step()
                    sp.dma_start(w_raw[:, s % 2, :],
                                 io["w"][layer * SLOTS + b * 6 + (s0 + 6 + s)]).then_inc(*sg.on(f"w_raw{s % 2}", ("ffn", s), 16))
                    if s in (1, 3):
                        j = s // 2
                        sp.wait_ge(*freed(layer, R0 + 4 + j, b * 12))
                        step()
                        sp.dma_start(io["o_ffn_new"][layer, b * 2 + (2 + j)],
                                     raw[:, j, SEQ:T + 2]).then_inc(*sg.on(f"ffn_stored{j}", "loop", 16))
            for j in range(2):
                sp.wait_ge(sg.sem(f"ffn_stored{j}"), layer * (16 * FB) + 16 * FB)
                step()
        for m in range(KD):
            sp.wait_ge(*sg.after("y_ready", m))
            step()
            sp.dma_start(io["y"][m], ev[:, m % 2, :]).then_inc(*sg.on(f"y_stored{m % 2}", m, 16))
        for kind in ("old_rows", "small_stored", "rows_stored", "ffn_stored0", "ffn_stored1", "y_stored0", "y_stored1"):
            sp.wait_ge(sg.sem(kind), (before or sg).count.get(kind, 16))
            step()

    @block.gpsimd
    def _(pool):
        pool.wait_ge(*sg.after("ones_ready"))
        pool.nop().then_inc(sg.sem("w_split_done"), FREE)
        with pool.Fori(0, DEPTH) as layer, sg.loop("layer", DEPTH, layer):
            with pool.Fori(0, SLOTS // 2) as i, sg.loop("split", SLOTS // 2, i):
                for q in range(2):
                    n = layer * (SLOTS // 2) + i
                    pool.wait_ge(sg.sem(f"w_raw{q}"), n * 16 + 16)
                    pool.wait_ge(sg.sem(f"w_used{q}"), n + FREE)
                    nc.gpsimd.tensor_tensor(w_hi[:, q, :], w_raw[:, q, :], ones[:, 0:1].to_broadcast([P, 1024]),
                                            ALU.mult).then_inc(sg.sem("w_hi_done"), 1)
                    pool.wait_ge(sg.sem("w_hi_done"), n * 2 + (q + 1))
                    nc.gpsimd.tensor_tensor(w_lo[:, q, :], w_raw[:, q, :], w_hi[:, q, :].bitcast(F32),
                                                 ALU.subtract).then_inc(*sg.on("w_split_done", q))

    @block.tensor
    def _(pe):
        mm = nc.tensor.matmul

        used = []

        def free_used(base=0):
            if used:
                q, r = used.pop()
                pe.wait_ge(sg.sem("m_ready"), layer * RUSES + base + (r + 1))
                pe.nop().then_inc(sg.sem(f"w_used{q}"), 1)

        def three(out, wh, wl, ah, al, first, last):
            for g in range(NG):
                c = slice(g * TG, (g + 1) * TG)
                mm(out[:, g, 0:TG], wh, ah[:, c], start=first, stop=False)
                mm(out[:, g, 0:TG], wh, al[:, c], start=False, stop=False)
                ins = mm(out[:, g, 0:TG], wl, ah[:, c], start=False, stop=last)
            return ins

        rg = Ring()
        ready = {}
        slot = [0]

        def in_half(m, half):
            if half == 0:
                pe.wait_ge(sg.sem("w_split_done"), layer * SLOTS + (slot[0] + 1 + FREE))
                m_r[0] = rg.next()
                pe.wait_ge(sg.sem("m_free"), layer * RUSES + (max(m_r[0] - 1, 0) + FREE))
            q = slot[0] % 2
            out = ring[:, m_r[0] % 2]
            for k in range(4 * half, 4 * half + 4):
                ins = three(out, w_hi[:, q, k * P:(k + 1) * P], w_lo[:, q, k * P:(k + 1) * P],
                            h_hi[:, k, :], h_lo[:, k, :], k == 0, k == KD - 1)
                free_used()
            if half == 1:
                ins.then_inc(*sg.on("m_ready", m_r[0]))
                used.append((q, m_r[0]))
                slot[0] += 1

        m_r = [0]

        def out_half(m, half):
            if half == 0:
                pe.wait_ge(sg.sem("w_split_done"), layer * SLOTS + (slot[0] + 1 + FREE))
            q = slot[0] % 2
            for mm_ in range(2 * half, 2 * half + 2):
                m_r[0] = rg.next()
                pe.wait_ge(sg.sem("m_free"), layer * RUSES + (max(m_r[0] - 1, 0) + FREE))
                out = ring[:, m_r[0] % 2]
                for k in range(2):
                    c = slice((mm_ * 2 + k) * P, (mm_ * 2 + k + 1) * P)
                    ins = three(out, w_hi[:, q, c], w_lo[:, q, c], y_hi[:, k, :], y_lo[:, k, :], k == 0, k == 1)
                    free_used()
                ins.then_inc(*sg.on("m_ready", m_r[0]))
            if half == 1:
                used.append((q, m_r[0]))
                slot[0] += 1

        def main(m, half):
            if m[0] == "in":
                in_half(m, half)
            else:
                if m[2] == 0 and half == 0:
                    pe.wait_ge(*sg.after("y_split", m[1]))
                out_half(m, half)

        def both(m):
            main(m, 0)
            main(m, 1)

        def run(halves):
            for m, half in halves:
                main(m, half)

        def norm(u, heads):
            uses = []
            for i, tiles in enumerate(heads):
                r = rg.next()
                uses.append(r)
                pe.wait_ge(sg.sem("m_free"), layer * RUSES + (max(r - 1, 0) + FREE))
                pe.wait_ge(*sg.after("sq_ready", (u, i)))
                for c in range(NCH + 1):
                    s = slice(c * CHUNK, min((c + 1) * CHUNK, T))
                    for k, t in enumerate(tiles):
                        ins = mm(ring[0:s.stop - s.start, r % 2, 2, 16 + c:17 + c], t[:, s], ones[:, 0:1],
                                 start=k == 0, stop=k == len(tiles) - 1)
                ins.then_inc(*sg.on("sq_turned", (u, i)))
            for i, r in enumerate(uses):
                pe.wait_ge(*sg.after("rms_ready", (u, i)))
                for c in range(NCH + 1):
                    n = min(CHUNK, T - c * CHUNK)
                    ins = mm(ring[:, r % 2, c // 4, (c % 4) * CHUNK:(c % 4) * CHUNK + n],
                             rms[0:n, i, c:c + 1].to_broadcast([n, P]), ident[0:n, 0:n], start=True, stop=True)
                ins.then_inc(*sg.on("m_ready", r))

        def ab_ready(u, c):
            if c > 0:
                pe.wait_ge(*sg.after("ab_free", (u, c)))
                return
            if u == 0:
                pe.wait_ge(*sg.after("cum_copied"))
            else:
                pe.wait_ge(*sg.after("gated", (u - 1, 1)))
            if u < 2:
                pe.wait_ge(*sg.after("silu", (u, 3)))
            else:
                pe.wait_ge(*sg.after("rope_done", u))
                pe.wait_ge(*sg.after("vg_loaded", (u, 5)))

        def stage1_s(u, c):
            s = cols(c)
            if c == 0:
                ab_ready(u, c)
            for h in range(4):
                da = tok[:, 1, 8 * c + 4 * u + h:8 * c + 4 * u + h + 1].to_broadcast([P, P])
                mm(ab[:, 1, h * 128:(h + 1) * 128], da, C("causal", 0, 128), start=True, stop=True)
            if c > 0:
                ab_ready(u, c)
            nc.tensor.transpose(ab[:, 0, 0:128], pt[:, 0, s], ident)
            nc.tensor.transpose(ab[:, 0, 128:256], pt[:, 2, s], ident)
            nc.tensor.transpose(ab[:, 0, 256:384], pt[:, 3, s], ident)
            mm(ab[:, 0, 384:512], pt[:, 0, s], pt[:, 1, s], start=True, stop=True).then_inc(*sg.on("stage1", (u, c)))

        def stage2_s(u, c):
            pe.wait_ge(*sg.after("mid_ready", (u, c)))
            for h in range(4):
                o = ab[64 * (h % 2):64 * (h % 2) + 64, 0, 128 * (h // 2):128 * (h // 2) + 128]
                mm(o, xtok[:, 64 * h:64 * h + 64], seg[:, 128 * h:128 * h + 128], start=True, stop=False)
                mm(o, St[:, 64 * h:64 * h + 64], Ce[:, 128 * h:128 * h + 128], start=False, stop=True)
            mm(ab[:, 0, 256:512], Btok, xw, start=True, stop=True).then_inc(*sg.on("stage2", (u, c)))

        def stage1_r(u, c):
            ab_ready(u, c)
            s = cols(c)
            nc.tensor.transpose(ab[:, 0, 0:128], pt[:, 2, s], ident)
            nc.tensor.transpose(ab[:, 0, 128:256], pt[:, 3, s], ident)
            nc.tensor.transpose(ab[:, 0, 256:384], pt[:, 1, s], ident)
            for h in range(2):
                r = slice(64 * h, 64 * h + 64)
                o = (ab[:, 1, 0:128], ab[:, 0, 384:512])[h]
                ins = mm(o, pt[r, 1, s], pt[r, 0, s], start=True, stop=True)
            ins.then_inc(*sg.on("stage1", (u, c)))

        def stage2_r(u, c):
            pe.wait_ge(*sg.after("mid_ready", (u, c)))
            for h in range(2):
                r = slice(64 * h, 64 * h + 64)
                o = ab[:, h, 0:128]
                mm(o, vtok[:, 128 * h:128 * h + 128], sT[:, 128 * h:128 * h + 128], start=True, stop=False)
                mm(o, St[r, 0:128], qd[r, :], start=False, stop=True)
            for h in range(2):
                ins = mm(ab[64 * h:64 * h + 64, 0, 256:384], kd[:, 64 * h:64 * h + 64],
                         vtok[:, 128 * h:128 * h + 128], start=True, stop=True)
            ins.then_inc(*sg.on("stage2", (u, c)))

        def decode_s(u):
            pe.wait_ge(*sg.after("ab_free", (u, NCH)))
            d = slice(SEQ, T)
            mm(ab[0:8, 0, 0:128], pt[:, 0, d], ident, start=True, stop=True)
            mm(ab[0:8, 0, 128:256], pt[:, 1, d], ident, start=True, stop=True)
            for w in range(2):
                for h in range(4):
                    v = tok[0:8, w, 64 + 4 * u + h:65 + 4 * u + h].to_broadcast([8, 64])
                    c0, r0 = 256 + 16 * w + 8 * (h // 2), 64 * (h % 2)
                    ins = mm(ab[r0:r0 + 64, 0, c0:c0 + 8], v, C("ident", 0, 8)[0:8], start=True, stop=True)
            ins.then_inc(*sg.on("dec_pe", (u, 0)))
            run(PLAN[u]["d0"])
            pe.wait_ge(*sg.after("dec_exp", u))
            for k in range(2):
                pe.wait_ge(*sg.after("dec_ready", (u, k)))
                for b in range(DEC):
                    ins = mm(abf[:, b * 128:(b + 1) * 128], C("sel", b * 128, 128)[0:8],
                             xtok[0:8, 128 * k:128 * k + 128], start=True, stop=True)
                ins.then_inc(*sg.on("dec_pe", (u, 1 + k)))
                run(PLAN[u][f"d{1 + k}"])

        def decode_r(u):
            pe.wait_ge(*sg.after("ab_free", (u, NCH)))
            d = slice(SEQ, T)
            mm(ab[0:8, 0, 0:128], pt[:, 2, d], ident, start=True, stop=True)
            mm(ab[0:8, 0, 128:256], pt[:, 3, d], ident, start=True, stop=True).then_inc(*sg.on("dec_pe", (u, 0)))
            pe.wait_ge(*sg.after("dec_ready", (u, 0)))
            for b in range(DEC):
                for h in range(2):
                    ins = mm(abf[64 * h:64 * h + 64, b * 128:(b + 1) * 128], C("sel", b * 128, 64)[0:8],
                             xtok[0:8, 128 * h:128 * h + 128], start=True, stop=True)
            ins.then_inc(*sg.on("dec_pe", (u, 1)))
            run(PLAN[u]["d0"])
            run(PLAN[u]["d1"])
            pe.wait_ge(*sg.after("dec_state_done", u))
            for h in range(2):
                for b in range(DEC):
                    r = slice(64 * h, 64 * h + 64)
                    ins = mm(ab[:, h, b:b + 1], raw[r, 0, b * 128:(b + 1) * 128],
                             pt[r, 0, SEQ + b:SEQ + b + 1], start=True, stop=True)
            ins.then_inc(*sg.on("dec_pe", (u, 2)))
            run(PLAN[u]["d2"])

        pe.wait_ge(*sg.after("const_loaded"))
        pe.wait_ge(*sg.after("ones_ready"))
        for q in range(2):
            pe.nop().then_inc(sg.sem(f"w_used{q}"), FREE)
        with pe.Fori(0, DEPTH) as layer, sg.loop("layer", DEPTH, layer):
            first_r = RING[FIRST[0]]
            pe.wait_ge(sg.sem("w_split_done"), layer * SLOTS + (1 + FREE))
            pe.wait_ge(sg.sem("m_free"), layer * RUSES + FREE)
            for k in range(KD):
                pe.wait_ge(sg.sem("h_split"), layer * (2 * KD) + (k + 1))
                three(ring[:, first_r % 2], w_hi[:, 0, k * P:(k + 1) * P], w_lo[:, 0, k * P:(k + 1) * P],
                      h_hi[:, k, :], h_lo[:, k, :], k == 0, k == KD - 1)
            slot[0] = 1
            for g in range(NG):
                ins = mm(ring[:, 0, g, 0:TG], ones[:], rstd[:, g * TG:(g + 1) * TG], start=True, stop=True)
            ins.then_inc(*sg.on("m_ready", RING["norm"]))
            pe.wait_ge(sg.sem("m_ready"), layer * RUSES + 1)
            pe.nop().then_inc(*sg.on("m_ready", first_r))
            used.append((0, first_r))
            rg.r = RING["dt"]
            r = rg.next()
            pe.wait_ge(sg.sem("m_free"), layer * RUSES + (r - 1 + FREE))
            pe.wait_ge(*sg.after("wdt_ready"))
            for k in range(KD):
                for g in range(NG):
                    ins = mm(ring[0:8, r % 2, g, 0:TG], wdt[:, 8 * k:8 * k + 8], x[:, k, g * TG:(g + 1) * TG],
                             start=k == 0, stop=k == KD - 1)
            ins.then_inc(*sg.on("m_ready", r))
            both(FIRST[1])
            pe.wait_ge(*freed(layer, RING["dt"]))
            for c in range(NCH):
                mm(ab[:, 0, 8 * c:8 * c + 8], pt[0:8, 0, cols(c)], ident[0:8, 0:8], start=True, stop=True)
            mm(ab[0:8, 0, 64:72], pt[0:8, 0, SEQ:T], ident[0:8, 0:8], start=True,
               stop=True).then_inc(*sg.on("dt_turned"))
            both(FIRST[2])
            pe.wait_ge(*sg.after("da_ready"))
            mm(ab[:, 0, 128:192], C("causal", 0, 128), tok[:, 1, 0:64], start=True,
               stop=True).then_inc(*sg.on("cum_done"))
            for m in FIRST[3:]:
                both(m)
            for u in range(4):
                s1, s2, dec = (stage1_s, stage2_s, decode_s) if u < 2 else (stage1_r, stage2_r, decode_r)
                at = PLAN[u]
                run(at["pre"])
                for c in range(NCH):
                    s1(u, c)
                    run(at[f"a{c}"])
                    s2(u, c)
                dec(u)
                norm(u, [[pt[:, 0, :], pt[:, 1, :]]] if u < 2 else [[pt[:, 0, :]], [pt[:, 1, :]]])
                run(at["fin"])
            for u in range(4, 6):
                at = PLAN[u]
                run(at["pre"])
                pe.wait_ge(*sg.after("gate_w_loaded", u))
                for j in range(2):
                    pe.wait_ge(*sg.after("conv_done", (u, j)))
                    for g in range(NG):
                        if (j, g) != (0, 0):
                            pe.wait_ge(*sg.after("sig", (u, j, g - 1) if g else (u, j - 1, NG - 1)))
                        elif u == 4:
                            pe.wait_ge(*sg.after("gated", (3, 1)))
                        else:
                            pe.wait_ge(*sg.after("sig", (u - 1, 1, NG - 1)))
                        c = slice(g * TG, (g + 1) * TG)
                        mm(ab[:, 0, 0:TG], gate_w[:, 2 * j, :], pt[:, j, c], start=True, stop=True)
                        mm(ab[:, 1, 0:TG], gate_w[:, 2 * j + 1, :], pt[:, j, c],
                           start=True, stop=True).then_inc(*sg.on("gates", (u, j, g)))
                    if j == 0:
                        run(at["g"])
                run(at["fin"])
            for m in LAST:
                both(m)
            assert (rg.r, slot[0], R0) == (RING["norm2"], 44, RING["norm2"] + 1)
            pe.wait_ge(sg.sem("w_split_done"), layer * SLOTS + (44 + 1 + FREE))
            pe.wait_ge(sg.sem("m_free"), layer * RUSES + (R0 - 1 + FREE))
            for k in range(KD):
                pe.wait_ge(sg.sem("h_split"), layer * (2 * KD) + (KD + k + 1))
                three(ring[:, R0 % 2], w_hi[:, 0, k * P:(k + 1) * P], w_lo[:, 0, k * P:(k + 1) * P],
                      h_hi[:, k, :], h_lo[:, k, :], k == 0, k == KD - 1)
                if k == 0:
                    pe.wait_ge(sg.sem("m_ready"), layer * RUSES + (R0 - 1))
                    pe.nop().then_inc(sg.sem("w_used1"), 1)
            for g in range(NG):
                ins = mm(ring[:, (R0 - 1) % 2, g, 0:TG], ones[:], rstd[:, g * TG:(g + 1) * TG],
                         start=True, stop=True)
            ins.then_inc(*sg.on("m_ready", RING["norm2"]))
            pe.wait_ge(sg.sem("m_ready"), layer * RUSES + R0)
            pe.nop().then_inc(*sg.on("m_ready", ("ffn", R0)))

            def ffn_slot(kind, q, r0, base, s, slot_base=0):
                pe.wait_ge(sg.sem("w_split_done"), layer * SLOTS + slot_base + (s + 1 + FREE))
                n = KD if kind == "up" else 2
                a, b_ = (h_hi, h_lo) if kind == "up" else (y_hi, y_lo)
                for i in range(1 if kind == "up" else 4):
                    r = r0 + i
                    pe.wait_ge(sg.sem("m_free"), layer * RUSES + base + (r - 1 + FREE))
                    for k in range(n):
                        c = slice((i * n + k) * P, (i * n + k + 1) * P)
                        ins = three(ring[:, r % 2], w_hi[:, q, c], w_lo[:, q, c], a[:, k, :], b_[:, k, :],
                                    k == 0, k == n - 1)
                        if i == k == 0:
                            pe.wait_ge(sg.sem("m_ready"), layer * RUSES + base + r0)
                            pe.nop().then_inc(sg.sem(f"w_used{1 - q}"), 1)
                    ins.then_inc(*sg.on("m_ready", ("ffn", r)))

            used.clear()
            for j in range(1, 4):
                ffn_slot("up", j % 2, R0 + j, 0, 44 + j)
            with pe.Fori(0, FB - 1) as b, sg.loop("ffn", FB - 1, b):
                for j in range(4):
                    ffn_slot("up", j % 2, R0 + 4 + j, b * 12, 48 + j, b * 6)
                pe.wait_ge(sg.sem("ffn_split"), layer * FB + (b + 1))
                for j in range(2):
                    ffn_slot("down", j, R0 + 8 + 4 * j, b * 12, 52 + j, b * 6)
            pe.wait_ge(sg.sem("ffn_split"), layer * FB + FB)
            for j in range(2):
                ffn_slot("down", j, R0 + 4 + 4 * j, 12 * (FB - 1), 48 + j, 6 * (FB - 1))
            pe.wait_ge(sg.sem("m_ready"), layer * RUSES + RUSES)
            pe.nop().then_inc(sg.sem("w_used1"), 1)
        pe.wait_ge(sg.sem("h_split"), (2 * DEPTH + 1) * KD)
        pe.wait_ge(sg.sem("m_free"), DEPTH * RUSES + FREE)
        for g in range(NG):
            ins = mm(ring[:, 0, g, 0:TG], ones[:], rstd[:, g * TG:(g + 1) * TG], start=True, stop=True)
        ins.then_inc(*sg.on("last_sum"))

    @block.scalar
    def _(act):
        af = nc.scalar.activation
        line = Line(sg, "act_line")

        def conv_tap(u, j, dst, src, w, b):
            act.wait_ge(*sg.after(f"raw_loaded{j % 2}", (u, j)))
            af(dst, src, ACT.Identity, bias=b, scale=w).then_inc(*sg.on("tap", (u, j)))

        def refresh(m, g, key):
            if m >= 2:
                act.wait_ge(*sg.after("sq_used", (key, m - 2)))
            af(ev[:, m % 2, :], x[:, m, :], ACT.Square).then_inc(*sg.on("sq_tile", (key, m)))
            af(h_hi[:, m, :], x[:, m, :], ACT.Identity, scale=gains[:, bass.ds(g * KD + m, 1)]
                    if not isinstance(g, int) else gains[:, g * KD + m:g * KD + m + 1]).then_inc(*sg.on("h_hi", (key, m)))

        def root(r, t):
            act.wait_ge(*freed(layer, r))
            af(t, t, ACT.Sqrt).then_inc(*sg.on("root", r))

        def y_free(u):
            if u > 0:
                act.wait_ge(sg.sem("m_ready"), layer * RUSES + (RING["out", u - 1, 1, 3] + 1))

        act.wait_ge(*sg.after("gains_loaded"))
        for m in range(KD):
            act.wait_ge(*sg.after(f"x_loaded{m}"))
            refresh(m, 0, "start")
        with act.Fori(0, DEPTH) as layer, sg.loop("layer", DEPTH, layer):
            root(RING["norm"], rstd[:])
            act.wait_ge(*sg.after("par_loaded"))
            af(rgc[:, :, 0], A("lam", 0, 4), ACT.Abs).then_inc(*line.step())
            act.wait_ge(*line.last())
            af(rgc[:, :, 1], rgc[:, :, 0], ACT.Exp, scale=-1.0).then_inc(*sg.on("lam_exp"))
            af(small[:, 0:8], A("a_log", 0, 8), ACT.Exp).then_inc(*sg.on("a_exp"))
            act.wait_ge(*sg.after("dt_in"))
            af(tok[:, 3, :], tok[:, 2, :], ACT.Abs).then_inc(*line.step())
            act.wait_ge(*line.last())
            af(tok[:, 3, :], tok[:, 3, :], ACT.Exp, scale=-1.0).then_inc(*sg.on("dt_exp"))
            for u in range(2):
                for j in range(4):
                    t = 4 * u + j
                    if u == 0 and j == 0:
                        act.wait_ge(*sg.after("dt_turned"))
                    conv_tap(u, j, pt[:, j, :], raw[:, j % 2, 3:T + 3], A("ssd_w", 4 * t + 3), A("ssd_b", t))
                for j in range(4):
                    act.wait_ge(*sg.after("conv_done", (u, j)))
                    af(pt[:, j, :], pt[:, j, :], ACT.Silu).then_inc(*sg.on("silu", (u, j)))
                act.wait_ge(*sg.after("gate_loaded", (u, 5)))
                af(pt[:, 4:6, :], pt[:, 4:6, :], ACT.Silu).then_inc(*sg.on("gate_act", u))
                for c in range(NCH):
                    act.wait_ge(*sg.after("seg_ready", (u, c)))
                    af(Ec, ab[:, 1, :], ACT.Exp).then_inc(*sg.on("Ec_ready", (u, c)))
                    af(seg, seg, ACT.Exp).then_inc(*sg.on("seg_exp", (u, c)))
                act.wait_ge(*sg.after("dec_ready", (u, 0)))
                af(small[:, 16:32], ab[:, 0, 272:288], ACT.Exp).then_inc(*sg.on("dec_exp", u))
                for j in range(2):
                    act.wait_ge(*sg.after("gated", (u, j)))
                    af(pt[:, j, :], pt[:, 2 + j, :],
                       ACT.Square).then_inc(*sg.on("sq_ready", (u, 0) if j else (u, "a")))
                act.wait_ge(*sg.after("ms_done", (u, 0)))
                af(rms[:, 0, :], rms[:, 0, :], ACT.Sqrt).then_inc(*sg.on("rms_root", (u, 0)))
                for j in range(2):
                    act.wait_ge(*sg.after("y_done", (u, j)))
                    y_free(u)
                    af(y_hi[:, j, :], pt[:, 2 + j, :], ACT.Identity).then_inc(*sg.on("y_hi", (u, j)))
            for u in range(2, 4):
                act.wait_ge(*sg.after("vg_loaded", (u, 5)))
                af(pt[:, 4:6, :], pt[:, 4:6, :], ACT.Silu).then_inc(*sg.on("gate_act", u))
                act.wait_ge(*sg.after("gated", (u, 1)))
                for j in range(2):
                    af(pt[:, j, :], pt[:, 2 + j, :], ACT.Square).then_inc(*sg.on("sq_ready", (u, j)))
                for j in range(2):
                    act.wait_ge(*sg.after("ms_done", (u, j)))
                    af(rms[:, j, :], rms[:, j, :], ACT.Sqrt).then_inc(*sg.on("rms_root", (u, j)))
                for j in range(2):
                    act.wait_ge(*sg.after("y_done", (u, j)))
                    y_free(u)
                    af(y_hi[:, j, :], pt[:, 2 + j, :], ACT.Identity).then_inc(*sg.on("y_hi", (u, j)))
            for u in range(4, 6):
                for j in range(2):
                    t = 2 * (u - 4) + j
                    conv_tap(u, j, pt[:, j, :], raw[:, j, 3:T + 3], A("lru_w", 4 * t + 3), A("lru_b", t))
                for j in range(2):
                    t = 2 * (u - 4) + j
                    for g in range(NG):
                        c = slice(g * TG, (g + 1) * TG)
                        act.wait_ge(*sg.after("gates", (u, j, g)))
                        af(pt[:, 2 + j, c], ab[:, 0, 0:TG], ACT.Sigmoid, bias=A("br", t))
                        af(pt[:, 4 + j, c], ab[:, 1, 0:TG], ACT.Sigmoid,
                           bias=A("bi", t)).then_inc(*sg.on("sig", (u, j, g)))
                act.wait_ge(*sg.after("lam_ready"))
                act.wait_ge(*sg.after("sig", (u, 1, 2)))
                for j in range(2):
                    t = 2 * (u - 4) + j
                    af((T0, T1)[j], pt[:, 2 + j, :], ACT.Tanh, scale=rgc[:, t, 3:4]).then_inc(*sg.on("tanh", (u, j)))
                    act.wait_ge(*sg.after("tanh", (u, j)))
                    af(pt[:, 2 + j, :], pt[:, 2 + j, :], ACT.Exp,
                       scale=rgc[:, t, 4:5]).then_inc(*sg.on("a_done", (u, j)))
                for j in range(2):
                    act.wait_ge(*sg.after("e_done", (u, j)))
                    af((T0, T1)[j], (T0, T1)[j], ACT.Sqrt).then_inc(*sg.on("lru_root", (u, j)))
                act.wait_ge(*sg.after("gate_loaded", (u, 3)))
                for j in range(2):
                    af(raw[:, j, 0:T], raw[:, j, 0:T], ACT.Gelu_apprx_tanh).then_inc(*sg.on("gelu", (u, j)))
                for j in range(2):
                    act.wait_ge(*sg.after("y_done", (u, j)))
                    y_free(u)
                    af(y_hi[:, j, :], pt[:, 4 + j, :], ACT.Identity).then_inc(*sg.on("y_hi", (u, j)))
            for q in range(2):
                act.wait_ge(*sg.after(f"ev_stored{q}", IN_TILES - 2 + q))
            for m in range(KD):
                act.wait_ge(*freed(layer, RING["out", 5, m // 4, m % 4]))
                refresh(m, layer * 2 + 1, "ffn")
            root(RING["norm2"], rstd[:])

            def ffn_block(blk, tag, base):
                for j in range(2):
                    act.wait_ge(*freed(layer, R0 + j, base))
                    wt = A_dyn(blk, j)
                    af(pt[:, j, :], raw[:, j, 2:T + 2], ACT.Identity, bias=wt[3],
                       scale=wt[2]).then_inc(*sg.on("ffn_tap", (tag, j)))
                for j in range(2):
                    act.wait_ge(*sg.after("ffn_conv", (tag, j)))
                    af(pt[:, j, :], pt[:, j, :], ACT.Gelu_apprx_tanh).then_inc(*sg.on("ffn_gelu", (tag, j)))
                for j in range(2):
                    act.wait_ge(*sg.after("ffn_y", (tag, j)))
                    af(y_hi[:, j, :], pt[:, 2 + j, :], ACT.Identity).then_inc(*sg.on("ffn_hi", (tag, j)))

            def A_dyn(blk, j):
                base = COL["ffn_w"]
                out = []
                for k in range(3):
                    out.append(pick(par, base, blk, 6, 3 * j + k))
                out.append(pick(par, COL["ffn_b"], blk, 2, j))
                return out

            ffn_block(0, "first", 0)
            with act.Fori(0, FB - 1) as b, sg.loop("ffn", FB - 1, b):
                ffn_block(b + 1, "loop", b * 12 + 4)
            for m in range(KD):
                act.wait_ge(*freed(layer, R0 + 4 + m, 12 * (FB - 1)))
                refresh(m, layer * 2 + 2, "next")
        act.wait_ge(*sg.after("last_ms"))
        af(rstd[:], rstd[:], ACT.Sqrt).then_inc(*sg.on("last_root"))

    @block.vector
    def _(dve):
        v = nc.vector
        line = Line(sg, "dve_line")
        stt = v.scalar_tensor_tensor
        rg = Ring()

        def refresh(m, g, key):
            dve.wait_ge(*sg.after("sq_tile", (key, m)))
            if m == 0:
                v.tensor_copy(rstd[:], ev[:, 0, :]).then_inc(*sg.on("sq_used", (key, 0)))
            else:
                dve.wait_ge(*sg.after("sq_used", (key, m - 1)))
                v.tensor_tensor(rstd[:], rstd[:], ev[:, m % 2, :], ALU.add).then_inc(*sg.on("sq_used", (key, m)))
            dve.wait_ge(*sg.after("h_hi", (key, m)))
            gp = gains[:, bass.ds(g * KD + m, 1)] if not isinstance(g, int) else gains[:, g * KD + m:g * KD + m + 1]
            stt(h_lo[:, m, :], x[:, m, :], gp, h_hi[:, m, :].bitcast(F32),
                ALU.mult, ALU.subtract).then_inc(sg.sem("h_split"), 1)

        def mean_square(dst, n, name):
            r = rg.next()
            assert r == RING[name]
            dve.wait_ge(sg.sem("m_ready"), layer * RUSES + (r + 1))
            v.tensor_scalar(g3(dst), ring[:, r % 2, :, 0:TG], 1.0 / n, EPS,
                            ALU.mult, ALU.add).then_inc(*sg.on("m_free", r))

        def unit_rms(u, i, n):
            r = rg.next()
            assert r == RING["norm", u, i]
            dve.wait_ge(*sg.after("sq_turned", (u, i)))
            v.tensor_scalar(rms[:, i, 0:NCH], ring[:, r % 2, 2, 16:16 + NCH], 1.0 / n, EPS, ALU.mult, ALU.add)
            v.tensor_scalar(rms[0:DEC, i, NCH:NCH + 1], ring[0:DEC, r % 2, 2, 16 + NCH:17 + NCH], 1.0 / n, EPS,
                            ALU.mult, ALU.add).then_inc(*sg.on("ms_done", (u, i)))
            dve.wait_ge(*sg.after("rms_root", (u, i)))
            v.reciprocal(rms[:, i, :], rms[:, i, :]).then_inc(*sg.on("rms_ready", (u, i)))
            return ring[:, r % 2].rearrange("p g n -> p (g n)")[:, 0:T]

        def root_inv(dst, name):
            dve.wait_ge(*sg.after("root", RING[name]))
            v.reciprocal(dst, dst).then_inc(*line.step())
            dve.wait_ge(*line.last())

        def conv(u, j, dst, src, w, prev, ntap):
            dve.wait_ge(*sg.after("tap", (u, j)))
            for k in range(ntap - 1):
                stt(dst[:, 0:SEQ], src[:, k:k + SEQ], w(k), dst[:, 0:SEQ], ALU.mult, ALU.add).then_inc(*line.step())
                dve.wait_ge(*line.last())
                ins = stt(dst[:, SEQ:T], prev(k), w(k), dst[:, SEQ:T], ALU.mult, ALU.add)
                if k < ntap - 2:
                    ins.then_inc(*line.step())
                    dve.wait_ge(*line.last())
            return ins

        def main(m, half):
            if m[0] == "in":
                if half == 1:
                    i = m[1]
                    r = rg.next()
                    dve.wait_ge(sg.sem("m_ready"), layer * RUSES + (r + 1))
                    if i >= 2:
                        dve.wait_ge(*sg.after(f"ev_stored{i % 2}", i - 2))
                    v.tensor_tensor(g3(ev[:, i % 2, :]), ring[:, r % 2, :, 0:TG], g3(rstd[:]),
                                    ALU.mult).then_inc(*sg.on("m_free", r))
            else:
                for i in range(2 * half, 2 * half + 2):
                    r = rg.next()
                    dve.wait_ge(sg.sem("m_ready"), layer * RUSES + (r + 1))
                    mo = 4 * m[2] + i
                    v.tensor_tensor(g3(x[:, mo, :]), ring[:, r % 2, :, 0:TG], g3(x[:, mo, :]),
                                    ALU.add).then_inc(*sg.on("m_free", r))
                    if m[1] == 5:
                        if mo > 0:
                            refresh(mo - 1, layer * 2 + 1, "ffn")
                        dve.wait_ge(*freed(layer, r))

        def both(m):
            main(m, 0)
            main(m, 1)

        def run(halves):
            for m, half in halves:
                main(m, half)

        v.memset(rms[:], 1.0).then_inc(*line.step())
        v.memset(ones[:], 1.0).then_inc(*sg.on("ones_ready"))
        dve.wait_ge(*line.last())
        v.nop().then_inc(sg.sem("m_free"), FREE)
        v.nop().then_inc(sg.sem("par_free"), FREE)
        dve.wait_ge(*sg.after("gains_loaded"))
        dve.wait_ge(*sg.after("const_loaded"))
        for m in range(KD):
            dve.wait_ge(*sg.after(f"x_loaded{m}"))
            refresh(m, 0, "start")
        with dve.Fori(0, DEPTH) as layer, sg.loop("layer", DEPTH, layer):
            dve.wait_ge(*sg.after("par_loaded"))
            v.tensor_tensor(wdt[:].rearrange("p (k h) -> p k h", h=SSD_H),
                                 A("wdt", 0, 64).rearrange("p (k h) -> p k h", h=SSD_H),
                                 gains[:, bass.ds(layer * (2 * KD), KD)].unsqueeze(2).to_broadcast([P, KD, SSD_H]),
                                 ALU.mult).then_inc(*sg.on("wdt_ready"))
            mean_square(rstd[:], D_MODEL, "norm")
            root_inv(rstd[:], "norm")
            both(FIRST[0])
            r = rg.next()
            dve.wait_ge(sg.sem("m_ready"), layer * RUSES + (r + 1))
            v.tensor_tensor(g3(pt[0:8, 0, :]), ring[0:8, r % 2, :, 0:TG], g3(rstd[0:8, :]),
                            ALU.mult).then_inc(*sg.on("m_free", r))
            both(FIRST[1])

            def log1p(e, s, s2, p):
                v.tensor_scalar(s, e, 2.0, None, ALU.add).then_inc(*line.step())
                dve.wait_ge(*line.last())
                v.reciprocal(s, s).then_inc(*line.step())
                dve.wait_ge(*line.last())
                v.tensor_tensor(s, s, e, ALU.mult).then_inc(*line.step())
                dve.wait_ge(*line.last())
                v.tensor_tensor(s2, s, s, ALU.mult).then_inc(*line.step())
                dve.wait_ge(*line.last())
                v.tensor_scalar(p, s2, 1.0 / 17, None, ALU.mult).then_inc(*line.step())
                dve.wait_ge(*line.last())
                for n in (15, 13, 11, 9, 7, 5, 3):
                    stt(p, p, 1.0 / n, s2, ALU.add, ALU.mult).then_inc(*line.step())
                    dve.wait_ge(*line.last())
                stt(p, p, 1.0, s, ALU.add, ALU.mult).then_inc(*line.step())
                dve.wait_ge(*line.last())
                v.tensor_scalar(p, p, 2.0, None, ALU.mult).then_inc(*line.step())
                dve.wait_ge(*line.last())

            dve.wait_ge(*sg.after("lam_exp"))
            log1p(rgc[:, :, 1], rgc[:, :, 2], rgc[:, :, 3], rgc[:, :, 4])
            v.tensor_scalar(rgc[:, :, 2], A("lam", 0, 4), -1.0, 0.0, ALU.mult, ALU.max).then_inc(*line.step())
            dve.wait_ge(*line.last())
            v.tensor_tensor(rgc[:, :, 2], rgc[:, :, 2], rgc[:, :, 4], ALU.add).then_inc(*line.step())
            dve.wait_ge(*line.last())
            v.tensor_scalar(rgc[:, :, 3], rgc[:, :, 2], 8.0, None, ALU.mult).then_inc(*line.step())
            dve.wait_ge(*line.last())
            v.tensor_scalar(rgc[:, :, 4], rgc[:, :, 2], -8.0, None, ALU.mult).then_inc(*sg.on("lam_ready"))
            dve.wait_ge(*sg.after("dt_turned"))
            v.memset(tok[:, 2, :], 0.0).then_inc(*line.step())
            dve.wait_ge(*line.last())
            bias = A("dt_bias", 0, 8)
            v.tensor_tensor(tok[:, 2, 0:64].rearrange("p (c h) -> p c h", h=8),
                                 ab[:, 0, 0:64].rearrange("p (c h) -> p c h", h=8),
                                 bias.unsqueeze(1).to_broadcast([P, 8, 8]), ALU.add).then_inc(*line.step())
            dve.wait_ge(*line.last())
            v.tensor_tensor(tok[0:8, 2, 64:72], ab[0:8, 0, 64:72], bias[0:8], ALU.add).then_inc(*sg.on("dt_in"))
            dve.wait_ge(*sg.after("dt_exp"))
            log1p(tok[:, 3, :], tok[:, 1, :], tok[:, 4, :], tok[:, 0, :])
            v.tensor_scalar(tok[:, 2, :], tok[:, 2, :], 0.0, None, ALU.max).then_inc(*line.step())
            dve.wait_ge(*line.last())
            v.tensor_tensor(tok[:, 0, :], tok[:, 0, :], tok[:, 2, :], ALU.add).then_inc(*line.step())
            dve.wait_ge(*line.last())
            dve.wait_ge(*sg.after("a_exp"))
            stt(tok[:, 1, :].rearrange("p (c h) -> p c h", h=8), tok[:, 0, :].rearrange("p (c h) -> p c h", h=8),
                     -1.0, small[:, 0:8].unsqueeze(1).to_broadcast([P, 9, 8]), ALU.mult, ALU.mult).then_inc(*sg.on("da_ready"))
            both(FIRST[2])
            dve.wait_ge(*sg.after("cum_done"))
            v.tensor_copy(tok[:, 2, 0:64], ab[:, 0, 128:192]).then_inc(*sg.on("cum_copied"))
            for m in FIRST[3:]:
                both(m)

            def split(u, j, src):
                dve.wait_ge(*sg.after("y_hi", (u, j)))
                ins = v.tensor_tensor(y_lo[:, j, :], src, y_hi[:, j, :].bitcast(F32), ALU.subtract)
                if j == 1:
                    ins.then_inc(*sg.on("y_split", u))

            for u in range(4):
                at = PLAN[u]
                if u < 2:
                    for j in range(2):
                        dve.wait_ge(*sg.after(f"raw_loaded{j}", (u, j)))
                        v.memset(raw[:, j, 0:3], 0.0).then_inc(*line.step())
                        dve.wait_ge(*line.last())
                    for j in range(4):
                        t = 4 * u + j
                        ins = conv(u, j, pt[:, j, :], raw[:, j % 2, :], lambda k: A("ssd_w", 4 * t + k),
                                   lambda k: A("ssd_prev", 24 * t + 8 * k, 8), LRU_W)
                        ins.then_inc(*sg.on("conv_done", (u, j)))
                        if j == 1:
                            run(at["pre"][:2])
                    run(at["pre"][2:])
                    dve.wait_ge(*sg.after("silu", (u, 3)))
                    v.memset(St, 0.0).then_inc(*line.step())
                    dve.wait_ge(*line.last())
                else:
                    dve.wait_ge(*sg.after("rope_loaded", (u, 1)))
                    for j in range(2):
                        dve.wait_ge(*sg.after("qk_loaded", (u, 1, 3)))
                        sc = 1.0 if j == 0 else RET_DK ** -0.5
                        stt(raw[:, j, 0:T], raw[:, j, 0:T], sc, T1, ALU.mult, ALU.mult)
                        stt(pt[:, j, :], pt[:, j, :], sc, T0, ALU.mult, ALU.mult).then_inc(*line.step())
                        dve.wait_ge(*line.last())
                        ins = v.tensor_tensor(pt[:, j, :], pt[:, j, :], raw[:, j, 0:T], ALU.add)
                        if j == 0:
                            ins.then_inc(*line.step())
                            dve.wait_ge(*line.last())
                            run(at["pre"][:2])
                        else:
                            ins.then_inc(*sg.on("rope_done", u))
                            dve.wait_ge(*sg.after("rope_done", u))
                    run(at["pre"][2:])
                    v.memset(St[:, 0:128], 0.0).then_inc(*line.step())
                    dve.wait_ge(*line.last())
                    dve.wait_ge(*sg.after("vg_loaded", (u, 5)))
                for c in range(NCH):
                    s = cols(c)
                    dve.wait_ge(*sg.after("stage1", (u, c)))
                    if u < 2:
                        ct = tok[:, 2, 8 * c + 4 * u:8 * c + 4 * u + 4]
                        dtt = tok[:, 0, 8 * c + 4 * u:8 * c + 4 * u + 4]
                        bb = ab[:, 1, :].rearrange("p (h i) -> p h i", h=4)
                        v.tensor_tensor(seg[:, 512:516], bb[:, :, 127], ct, ALU.subtract)
                        for h in range(4):
                            ins = v.tensor_scalar(seg[:, 128 * h:128 * h + 128], bb[:, h, :], ct[:, h:h + 1], 0.0,
                                                  ALU.subtract, ALU.min)
                        ins.then_inc(*sg.on("seg_ready", (u, c)))
                        v.tensor_copy(ch[:, 0:384], ab[:, 0, 0:384])
                        v.tensor_tensor(cbm, ab[:, 0, 384:512], C("causal", 0, 128), ALU.mult).then_inc(*line.step())
                        dve.wait_ge(*line.last())
                        dve.wait_ge(*sg.after("Ec_ready", (u, c)))
                        v.tensor_tensor(Ce.rearrange("p (h i) -> p h i", h=4), Ec.rearrange("p (h i) -> p h i", h=4),
                                        pt[:, 1, s].unsqueeze(1).to_broadcast([P, 4, 128]), ALU.mult)
                        dve.wait_ge(*sg.after("seg_exp", (u, c)))
                        v.tensor_tensor(seg[:, 512:516], seg[:, 512:516], dtt, ALU.mult).then_inc(*line.step())
                        dve.wait_ge(*line.last())
                        v.tensor_tensor(xw.rearrange("p (h d) -> p h d", h=4), xtok.rearrange("p (h d) -> p h d", h=4),
                                        seg[:, 512:516].unsqueeze(2).to_broadcast([P, 4, 64]), ALU.mult)
                        for h in range(4):
                            e = seg[:, 128 * h:128 * h + 128]
                            ins = stt(e, e, dtt[:, h:h + 1], cbm, ALU.mult, ALU.mult)
                        ins.then_inc(*sg.on("mid_ready", (u, c)))
                        run(at[f"a{c}"])
                        dve.wait_ge(*sg.after("stage2", (u, c)))
                        for j in range(2):
                            ins = stt(pt[:, 2 + j, s], pt[:, 2 + j, s], A("ssd_d", 2 * u + j),
                                      ab[:, 0, 128 * j:128 * j + 128], ALU.mult, ALU.add)
                        s4 = St.rearrange("p (h d) -> p h d", h=4)
                        el = Ec.rearrange("p (h i) -> p h i", h=4)[:, :, 127:128].to_broadcast([P, 4, 64])
                        v.tensor_tensor(s4, s4, el, ALU.mult).then_inc(*line.step())
                        dve.wait_ge(*line.last())
                        v.tensor_tensor(St, St, ab[:, 0, 256:512], ALU.add).then_inc(*sg.on("ab_free", (u, c + 1)))
                    else:
                        g = u - 2
                        v.tensor_copy(vtok, ab[:, 0, 0:256])
                        v.tensor_tensor(kd.rearrange("p (h d) -> p h d", h=2),
                                        ab[:, 0, 256:384].rearrange("p (h d) -> p h d", h=2),
                                        C("kdec", 2 * g, 2).unsqueeze(2).to_broadcast([P, 2, 64]), ALU.mult)
                        v.tensor_tensor(sT[:, 0:128], ab[:, 1, 0:128], C("decay", 256 * g, 128), ALU.mult)
                        v.tensor_tensor(sT[:, 128:256], ab[:, 0, 384:512], C("decay", 256 * g + 128, 128), ALU.mult)
                        v.tensor_tensor(qd, pt[:, 0, s], C("qdec", 128 * g, 128),
                                        ALU.mult).then_inc(*sg.on("mid_ready", (u, c)))
                        run(at[f"a{c}"])
                        dve.wait_ge(*sg.after("stage2", (u, c)))
                        v.tensor_copy(pt[:, 2:4, s], ab[:, :, 0:128])
                        stt(St[:, 0:128], St[:, 0:128], C("cdec", g), ab[:, 0, 256:384], ALU.mult,
                            ALU.add).then_inc(*sg.on("ab_free", (u, c + 1)))
                d = slice(SEQ, T)
                dve.wait_ge(*sg.after("dec_pe", (u, 0)))
                if u < 2:
                    v.tensor_copy(xtok[0:8, 0:256], ab[0:8, 0, 0:256])
                    xdt = small[:, 32:48].rearrange("p (j b) -> p j b", j=2)
                    v.tensor_tensor(xdt, ab[:, 0, 256:272].rearrange("p (j b) -> p j b", j=2), pt[:, 2:4, d],
                                    ALU.mult).then_inc(*sg.on("dec_ready", (u, 0)))
                    dve.wait_ge(*sg.after("dec_loaded", u))
                    rf = raw[:].rearrange("p a n -> p (a n)")[:, 0:2048].rearrange("p (j b n) -> p j b n", j=2, b=DEC)
                    dve.wait_ge(*sg.after("small_stored", (u, 0)))
                    work = ch[:, 384:384 + 2048].rearrange("p (j b n) -> p j b n", j=2, b=DEC)
                    dve.wait_ge(*sg.after("dec_exp", u))
                    for j in range(2):
                        ed = small[:, 16 + 8 * j:24 + 8 * j].unsqueeze(2).to_broadcast([P, DEC, 128])
                        v.tensor_tensor(rf[:, j], rf[:, j], ed, ALU.mult)
                    run(at["d0"])
                    dve.wait_ge(*sg.after("dec_pe", (u, 1)))
                    bbc = abf.rearrange("p (b n) -> p b n", b=DEC)
                    for j in range(2):
                        xb = xdt[:, j].unsqueeze(2).to_broadcast([P, DEC, 128])
                        ins = v.tensor_tensor(work[:, j], bbc, xb, ALU.mult)
                    ins.then_inc(*sg.on("dec_ready", (u, 1)))
                    dve.wait_ge(*sg.after("dec_ready", (u, 1)))
                    for j in range(2):
                        ins = v.tensor_tensor(rf[:, j], rf[:, j], work[:, j], ALU.add)
                    ins.then_inc(*sg.on("dec_state_done", u))
                    run(at["d1"])
                    dve.wait_ge(*sg.after("dec_state_done", u))
                    dve.wait_ge(*sg.after("dec_pe", (u, 2)))
                    for j in range(2):
                        ins = v.tensor_tensor(work[:, j], rf[:, j], bbc, ALU.mult)
                    ins.then_inc(*line.step())
                    dve.wait_ge(*line.last())
                    run(at["d2"])
                    v.tensor_reduce(small[:, 48:64].rearrange("p (j b) -> p j b", j=2), work, AX_X,
                                    ALU.add).then_inc(*line.step())
                    dve.wait_ge(*line.last())
                    for j in range(2):
                        stt(pt[:, 2 + j, d], pt[:, 2 + j, d], A("ssd_d", 2 * u + j), small[:, 48 + 8 * j:56 + 8 * j],
                                 ALU.mult, ALU.add).then_inc(*line.step())
                        dve.wait_ge(*line.last())
                    dve.wait_ge(*sg.after("gate_act", u))
                    for j in range(2):
                        v.tensor_tensor(pt[:, 2 + j, :], pt[:, 2 + j, :], pt[:, 4 + j, :],
                                        ALU.mult).then_inc(*sg.on("gated", (u, j)))
                    inv = unit_rms(u, 0, 256)
                    dve.wait_ge(sg.sem("m_ready"), layer * RUSES + (RING["norm", u, 0] + 1))
                    for j in range(2):
                        stt(pt[:, 2 + j, :], pt[:, 2 + j, :], A("ssd_g", 2 * u + j), inv,
                            ALU.mult, ALU.mult).then_inc(*sg.on("y_done", (u, j)))
                    dve.wait_ge(*sg.after("y_done", (u, 1)))
                    v.nop().then_inc(*sg.on("m_free", RING["norm", u, 0]))
                    run(at["fin"][:2])
                else:
                    g = u - 2
                    v.tensor_copy(xtok[0:8, 0:256], ab[0:8, 0, 0:256]).then_inc(*sg.on("dec_ready", (u, 0)))
                    dve.wait_ge(*sg.after("dec_loaded", u))
                    st = raw[:, 0, 0:1024].rearrange("p (b n) -> p b n", b=DEC)
                    work = raw[:, 1, 0:1024].rearrange("p (b n) -> p b n", b=DEC)
                    dve.wait_ge(*sg.after("dec_pe", (u, 1)))
                    v.tensor_tensor(work, abf.rearrange("p (b n) -> p b n", b=DEC),
                                         pt[:, 1, d].unsqueeze(2).to_broadcast([P, DEC, 128]), ALU.mult).then_inc(*line.step())
                    dve.wait_ge(*line.last())
                    stt(raw[:, 0, 0:1024], raw[:, 0, 0:1024], C("gamma", g), raw[:, 1, 0:1024], ALU.mult,
                        ALU.add).then_inc(*sg.on("dec_state_done", u))
                    run(at["d0"])
                    run(at["d1"])
                    dve.wait_ge(*sg.after("dec_pe", (u, 2)))
                    v.tensor_copy(pt[:, 2:4, d], ab[:, :, 0:DEC]).then_inc(*sg.on("gated", (u, 1)))
                    run(at["d2"])
                    dve.wait_ge(*sg.after("small_stored", (u, 1)))
                    dve.wait_ge(*sg.after("gate_act", u))
                    inv = [unit_rms(u, j, RET_DV) for j in range(2)]
                    for j in range(2):
                        dve.wait_ge(sg.sem("m_ready"), layer * RUSES + (RING["norm", u, j] + 1))
                        stt(pt[:, 2 + j, :], pt[:, 2 + j, :], A("ret_g", 2 * g + j), inv[j],
                            ALU.mult, ALU.mult).then_inc(*sg.on("m_free", RING["norm", u, j]))
                        dve.wait_ge(sg.sem("m_free"), layer * RUSES + (RING["norm", u, j] + 1 + FREE))
                        v.tensor_tensor(pt[:, 2 + j, :], pt[:, 2 + j, :], pt[:, 4 + j, :],
                                        ALU.mult).then_inc(*sg.on("y_done", (u, j)))
                    run(at["fin"][:2])
                run(at["fin"][2:])
                for j in range(2):
                    split(u, j, pt[:, 2 + j, :])
            for u in range(4, 6):
                at = PLAN[u]
                for j in range(2):
                    t = 2 * (u - 4) + j
                    dve.wait_ge(*sg.after(f"raw_loaded{j}", (u, j)))
                    v.memset(raw[:, j, 0:3], 0.0).then_inc(*line.step())
                    dve.wait_ge(*line.last())
                    ins = conv(u, j, pt[:, j, :], raw[:, j, :], lambda k: A("lru_w", 4 * t + k),
                               lambda k: A("lru_prev", 24 * t + 8 * k, 8), LRU_W)
                    ins.then_inc(*sg.on("conv_done", (u, j)))
                    if j == 0:
                        run(at["pre"][:2])
                run(at["pre"][2:])
                run(at["g"])
                for j in range(2):
                    dve.wait_ge(*sg.after("sig", (u, j, 2)))
                    v.tensor_tensor(pt[:, 4 + j, :], pt[:, 4 + j, :], pt[:, j, :], ALU.mult).then_inc(*line.step())
                    dve.wait_ge(*line.last())
                for j in range(2):
                    t = 2 * (u - 4) + j
                    dve.wait_ge(*sg.after("a_done", (u, j)))
                    v.tensor_tensor(pt[:, j, :], pt[:, 2 + j, :], pt[:, 2 + j, :], ALU.mult).then_inc(*line.step())
                    dve.wait_ge(*line.last())
                    stt((T0, T1)[j], pt[:, j, :], 1.0, (T0, T1)[j], ALU.add,
                        ALU.mult).then_inc(*sg.on("e_done", (u, j)))
                run(at["fin"][:2])
                for j in range(2):
                    t = 2 * (u - 4) + j
                    dve.wait_ge(*sg.after("lru_root", (u, j)))
                    v.tensor_tensor(pt[:, 4 + j, :], pt[:, 4 + j, :], (T0, T1)[j], ALU.mult).then_inc(*line.step())
                    dve.wait_ge(*line.last())
                    d = slice(SEQ, T)
                    v.tensor_tensor_scan(pt[:, j, 0:SEQ], pt[:, 2 + j, 0:SEQ], pt[:, 4 + j, 0:SEQ], 0.0,
                                              ALU.mult, ALU.add).then_inc(*line.step())
                    dve.wait_ge(*line.last())
                    v.tensor_tensor(pt[:, j, d], pt[:, 2 + j, d], A("lru_h0", 8 * t, 8),
                                    ALU.mult).then_inc(*line.step())
                    dve.wait_ge(*line.last())
                    v.tensor_tensor(pt[:, j, d], pt[:, j, d], pt[:, 4 + j, d],
                                    ALU.add).then_inc(*sg.on("h_done", (u, j)))
                for j in range(2):
                    dve.wait_ge(*sg.after("h_done", (u, j)))
                    dve.wait_ge(*sg.after("gelu", (u, j)))
                    v.tensor_tensor(pt[:, 4 + j, :], pt[:, j, :], raw[:, j, 0:T],
                                    ALU.mult).then_inc(*sg.on("y_done", (u, j)))
                run(at["fin"][2:])
                for j in range(2):
                    split(u, j, pt[:, 4 + j, :])
            for m in LAST:
                both(m)
            refresh(KD - 1, layer * 2 + 1, "ffn")
            mean_square(rstd[:], D_MODEL, "norm2")
            root_inv(rstd[:], "norm2")
            for j in range(2):
                v.memset(raw[:, j, 0:2], 0.0).then_inc(*line.step())
                dve.wait_ge(*line.last())

            def up_part(blk, tag, r0, base):
                for j in range(2):
                    r = r0 + j
                    dve.wait_ge(sg.sem("m_ready"), layer * RUSES + base + (r + 1))
                    if tag == "loop":
                        dve.wait_ge(sg.sem(f"ffn_stored{j}"), layer * (16 * FB) + (b + 1) * 16)
                    v.tensor_tensor(g3(raw[:, j, 2:T + 2]), ring[:, r % 2, :, 0:TG], g3(rstd[:]),
                                    ALU.mult).then_inc(*sg.on("m_free", ("ffn", r)))
                for j in range(2):
                    dve.wait_ge(*sg.after("ffn_tap", (tag, j)))
                    for k in range(2):
                        w = pick(par, COL["ffn_w"], blk, 6, 3 * j + k)
                        pv = pick(par, COL["ffn_prev"], blk, 32, 16 * j + 8 * k, 8)
                        stt(pt[:, j, 0:SEQ], raw[:, j, k:k + SEQ], w, pt[:, j, 0:SEQ], ALU.mult,
                            ALU.add).then_inc(*line.step())
                        dve.wait_ge(*line.last())
                        ins = stt(pt[:, j, SEQ:T], pv, w, pt[:, j, SEQ:T], ALU.mult, ALU.add)
                        if k == 0:
                            ins.then_inc(*line.step())
                            dve.wait_ge(*line.last())
                    ins.then_inc(*sg.on("ffn_conv", (tag, j)))
                for j in range(2):
                    r = r0 + 2 + j
                    dve.wait_ge(sg.sem("m_ready"), layer * RUSES + base + (r + 1))
                    v.tensor_tensor(g3(pt[:, 2 + j, :]), ring[:, r % 2, :, 0:TG], g3(rstd[:]),
                                    ALU.mult).then_inc(*sg.on("m_free", ("ffn", r)))

            def y_part(tag, r, base):
                dve.wait_ge(*freed(layer, r, base))
                for j in range(2):
                    dve.wait_ge(*sg.after("ffn_gelu", (tag, j)))
                    v.tensor_tensor(pt[:, 2 + j, :], pt[:, 2 + j, :], pt[:, j, :],
                                    ALU.mult).then_inc(*sg.on("ffn_y", (tag, j)))
                for j in range(2):
                    dve.wait_ge(*sg.after("ffn_hi", (tag, j)))
                    ins = v.tensor_tensor(y_lo[:, j, :], pt[:, 2 + j, :], y_hi[:, j, :].bitcast(F32), ALU.subtract)
                ins.then_inc(*sg.on("ffn_split", tag))

            up_part(0, "first", R0, 0)
            y_part("first", R0 + 3, 0)
            with dve.Fori(0, FB - 1) as b, sg.loop("ffn", FB - 1, b):
                up_part(b + 1, "loop", R0 + 4, b * 12)
                for mo in range(KD):
                    r = R0 + 8 + mo
                    dve.wait_ge(sg.sem("m_ready"), layer * RUSES + b * 12 + (r + 1))
                    v.tensor_tensor(g3(x[:, mo, :]), ring[:, r % 2, :, 0:TG], g3(x[:, mo, :]),
                                    ALU.add).then_inc(*sg.on("m_free", ("ffn", r)))
                y_part("loop", R0 + 7, b * 12)
            dve.wait_ge(*sg.after("ffn_split", "loop"))
            v.nop().then_inc(*sg.on("par_free"))
            for mo in range(KD):
                r = R0 + 4 + mo
                dve.wait_ge(sg.sem("m_ready"), layer * RUSES + 12 * (FB - 1) + (r + 1))
                v.tensor_tensor(g3(x[:, mo, :]), ring[:, r % 2, :, 0:TG], g3(x[:, mo, :]),
                                ALU.add).then_inc(*sg.on("m_free", ("last", r)))
                if mo >= 1:
                    refresh(mo - 1, layer * 2 + 2, "next")
            refresh(KD - 1, layer * 2 + 2, "next")
        dve.wait_ge(*sg.after("last_sum"))
        v.tensor_scalar(g3(rstd[:]), ring[:, 0, :, 0:TG], 1.0 / D_MODEL, EPS, ALU.mult,
                        ALU.add).then_inc(*sg.on("last_ms"))
        dve.wait_ge(*sg.after("last_root"))
        v.reciprocal(rstd[:], rstd[:]).then_inc(*sg.on("last_rstd"))
        dve.wait_ge(*sg.after("last_rstd"))
        for m in range(KD):
            if m >= 2:
                dve.wait_ge(*sg.after(f"y_stored{m % 2}", m - 2))
            stt(ev[:, m % 2, :], x[:, m, :], gains[:, 2 * DEPTH * KD + m:2 * DEPTH * KD + m + 1], rstd[:],
                     ALU.mult, ALU.mult).then_inc(*sg.on("y_ready", m))
    return sg


def constants():
    f8 = np.float64
    log_g = np.log1p(-np.exp2(-5.0 - np.arange(RET_H, dtype=f8)))
    i = np.arange(CHUNK, dtype=f8)
    con = np.zeros((P, NCON), np.float32)

    def put(name, a):
        a = np.asarray(a, np.float32)
        con[:a.shape[0], CON[name]:CON[name] + a.shape[1]] = a
    put("ident", np.eye(P))
    causal = (i[:, None] <= i[None, :])
    put("causal", causal)
    for h in range(RET_H):
        con[:, CON["decay"] + h * 128:CON["decay"] + (h + 1) * 128] = \
            np.where(causal, np.exp(np.maximum(i[None, :] - i[:, None], 0) * log_g[h]), 0)
        con[:, CON["kdec"] + h] = np.exp((CHUNK - 1.0 - i) * log_g[h])
        rows = slice(64 * (h % 2), 64 * (h % 2) + 64)
        c = CON["qdec"] + 128 * (h // 2)
        con[rows, c:c + 128] = np.exp((i + 1.0) * log_g[h])[None, :]
        con[rows, CON["cdec"] + h // 2] = np.exp(CHUNK * log_g[h])
        con[rows, CON["gamma"] + h // 2] = np.exp(log_g[h])
    for b in range(8):
        con[b, CON["sel"] + b * 128:CON["sel"] + (b + 1) * 128] = 1
    half = RET_DK // 2
    freqs = np.float32(10000.0) ** (-np.arange(half, dtype=np.float32) / np.float32(half))
    pos = np.concatenate([np.arange(SEQ), np.full(DEC, PAST_LEN)]).astype(np.float32)
    ang = (freqs[:, None] * pos[None, :]).astype(np.float32).astype(f8)
    cos = np.tile(np.cos(ang), (4, 1)).astype(np.float32)
    sin = np.tile(np.concatenate([-np.sin(ang), np.sin(ang)]), (2, 1)).astype(np.float32)
    return con, cos, sin


def feature_cols():
    lx, lg, rq, rk, rv, rgt, z, xbc, dt = np.cumsum([0, 512, 512, 256, 256, 512, 512, 512, 1024])
    xs, bm, cm = xbc, xbc + 512, xbc + 768
    starts = []
    for g in range(2):
        starts += [bm + 128 * g, cm + 128 * g, xs + 256 * g, xs + 256 * g + 128, z + 256 * g, z + 256 * g + 128]
    for g in range(2):
        starts += [rq + 128 * g, rk + 128 * g, rv + 256 * g, rv + 256 * g + 128, rgt + 256 * g, rgt + 256 * g + 128]
    for p in range(2):
        starts += [lx + 256 * p, lx + 256 * p + 128, lg + 256 * p, lg + 256 * p + 128]
    return starts, int(dt)


def lay_out(i):
    f = np.float32
    L = DEPTH
    d = {}
    x = np.concatenate([i["x_prompt"][0], i["x_sample"][:, 0]], axis=0)
    d["x"] = x.T.reshape(KD, P, T)
    starts, dt0 = feature_cols()
    w = np.zeros((L, SLOTS, P, 1024), f)

    def up_slot(wm, c0):
        return wm[:, c0:c0 + P].reshape(KD, P, P).transpose(1, 0, 2).reshape(P, 1024)

    def down_slot(wm, rows, half):
        a = wm[rows[0]:rows[0] + P], wm[rows[1]:rows[1] + P]
        a = np.stack([t[:, 512 * half:512 * half + 512].reshape(P, 4, P) for t in a], axis=2)
        return a.reshape(P, 1024)
    mix0 = [1024, 1280, 512, 768, 0, 256]
    for l in range(L):
        for s, m in enumerate(ORDER):
            if m[0] == "in":
                w[l, s] = up_slot(i["w_in"][l], starts[m[1]])
            else:
                r = mix0[m[1]]
                w[l, s] = down_slot(i["w_out"][l], (r, r + P), m[2])
        s = len(ORDER)
        up, down = i["ffn_w_up"][l], i["ffn_w_down"][l]

        def ups(b):
            return [up_slot(up, c) for c in (256 * b, 256 * b + 128, D_FF + 256 * b, D_FF + 256 * b + 128)]

        def downs(b):
            return [down_slot(down, (256 * b, 256 * b + 128), h) for h in range(2)]
        seq = ups(0)
        for b in range(FB - 1):
            seq += ups(b + 1) + downs(b)
        seq += downs(FB - 1)
        w[l, s:] = np.stack(seq)
    d["w"] = w.reshape(L * SLOTS, P, 1024)
    par = np.zeros((L, P, NPAR), f)

    def put(l, name, a):
        par[l, :a.shape[0], COL[name]:COL[name] + a.shape[1]] = a

    def tiles(v):
        return v.reshape(-1, P).T

    def taps(wc, order):
        return np.concatenate([wc[:, c:c + P].T for c in order], axis=1)

    def past(st, order):
        return np.concatenate([st[:, :, c:c + P].transpose(2, 1, 0).reshape(P, -1) for c in order], axis=1)
    so = []
    for g in range(2):
        so += [512 + 128 * g, 768 + 128 * g, 256 * g, 256 * g + 128]
    lo = [0, 128, 256, 384]
    fo = [128 * n for n in range(FT)]
    for l in range(L):
        put(l, "lru_w", taps(i["lru_conv_w"][l], lo))
        put(l, "lru_b", tiles(i["lru_conv_b"][l]))
        put(l, "br", tiles(i["lru_br"][l]))
        put(l, "bi", tiles(i["lru_bi"][l]))
        put(l, "lam", tiles(i["lru_lambda"][l]))
        put(l, "ret_g", i["ret_norm_g"][l].T)
        put(l, "ssd_w", taps(i["ssd_conv_w"][l], so))
        put(l, "ssd_b", np.stack([i["ssd_conv_b"][l][c:c + P] for c in so], axis=1))
        put(l, "ssd_d", tiles(np.repeat(i["ssd_d"][l], 64)))
        put(l, "ssd_g", tiles(i["ssd_norm_g"][l]))
        put(l, "dt_bias", np.broadcast_to(i["ssd_dt_bias"][l], (P, 8)))
        put(l, "a_log", np.broadcast_to(i["ssd_a_log"][l], (P, 8)))
        put(l, "ffn_w", taps(i["ffn_conv_w"][l], fo))
        put(l, "ffn_b", tiles(i["ffn_conv_b"][l]))
        put(l, "lru_h0", np.concatenate([i["state_lru_h"][l][:, c:c + P].T for c in lo], axis=1))
        put(l, "lru_prev", past(i["state_lru_conv"][l], lo))
        put(l, "ssd_prev", past(i["state_ssd_conv"][l], so))
        put(l, "ffn_prev", past(i["state_ffn_conv"][l], fo))
        put(l, "wdt", i["w_in"][l][:, dt0:dt0 + 8].reshape(KD, P, 8).transpose(1, 0, 2).reshape(P, 64))
    d["par"] = par
    g = []
    for l in range(L):
        g += [tiles(i["norm_mix_g"][l]), tiles(i["norm_ffn_g"][l])]
    d["gains"] = np.concatenate(g + [tiles(i["norm_final_g"])], axis=1)
    gw = np.zeros((L, 2, P, 4, P), f)
    for l in range(L):
        for t in range(4):
            for n, name in enumerate(("lru_wr", "lru_wi")):
                for q in range(2):
                    s = slice(64 * q, 64 * q + 64)
                    gw[l, t // 2, s, 2 * (t % 2) + n, s] = i[name][l, 2 * t + q]
    d["gate_w"] = gw
    d["ret_state"] = i["state_ret"].reshape(L, 8, 2, 2, 64, 128).transpose(0, 2, 3, 4, 1, 5).reshape(L, 2, P, 1024)
    d["ssd_state"] = i["state_ssd"].reshape(L, 8, 2, 2, 2, 64, 128).transpose(0, 2, 4, 5, 3, 1, 6).reshape(L, 2, P, 2, 1024)
    d["i_lru_old"] = i["state_lru_conv"][:, :, 1:]
    d["i_ssd_old"] = i["state_ssd_conv"][:, :, 1:]
    d["i_ffn_old"] = i["state_ffn_conv"][:, :, 1:]
    d["con"], d["cos"], d["sin"] = constants()
    return {k: np.ascontiguousarray(a, dtype=f) for k, a in d.items()}


OUTS = {
    "y": (KD, P, T),
    "o_lru_old": (DEPTH, 8, 2, 512), "o_ssd_old": (DEPTH, 8, 2, 1024), "o_ffn_old": (DEPTH, 8, 1, D_FF),
    "o_lru_new": (DEPTH, 4, P, 11), "o_ssd_new": (DEPTH, 8, P, 11), "o_ffn_new": (DEPTH, FT, P, 10),
    "o_lru_h": (DEPTH, 4, P, 9),
    "o_ret_p": (DEPTH, 2, P, 128), "o_ret_s": (DEPTH, 2, P, 1024),
    "o_ssd_p": (DEPTH, 2, P, 256), "o_ssd_s": (DEPTH, 2, P, 2, 1024),
}


def give_back(r):
    L = DEPTH
    y = r["y"].reshape(D_MODEL, T).T
    y_p, y_s = y[None, :SEQ], y[SEQ:, None]

    def conv_state(new, old, order, n):
        width = new.shape[1] * P
        at = np.argsort(order)
        a = new[:, at].reshape(L, width, -1)
        p = a[:, :, :n].transpose(0, 2, 1)[:, None]
        s = np.concatenate([old, a[:, :, n:].transpose(0, 2, 1)[:, :, None]], axis=2)
        return p, s
    so = []
    for g in range(2):
        so += [512 + 128 * g, 768 + 128 * g, 256 * g, 256 * g + 128]
    lc_p, lc_s = conv_state(r["o_lru_new"], r["o_lru_old"], range(4), 3)
    sc_p, sc_s = conv_state(r["o_ssd_new"], r["o_ssd_old"], so, 3)
    fc_p, fc_s = conv_state(r["o_ffn_new"], r["o_ffn_old"], range(FT), 2)
    h = r["o_lru_h"].reshape(L, 512, 9)
    h_p, h_s = h[:, :, 0][:, None], h[:, :, 1:].transpose(0, 2, 1)
    ret_p = r["o_ret_p"].reshape(L, 1, 4, 64, 128)
    ret_s = r["o_ret_s"].reshape(L, 2, 2, 64, 8, 128).transpose(0, 4, 1, 2, 3, 5).reshape(L, 8, 4, 64, 128)
    ssd_p = r["o_ssd_p"].reshape(L, 2, P, 4, 64).transpose(0, 1, 3, 4, 2).reshape(L, 1, 8, 64, 128)
    ssd_s = r["o_ssd_s"].reshape(L, 2, 2, 64, 2, 8, 128).transpose(0, 5, 1, 4, 2, 3, 6).reshape(L, 8, 8, 64, 128)
    out = (y_p, y_s, lc_p, lc_s, h_p, h_s, ret_p, ret_s, sc_p, sc_s, ssd_p, ssd_s, fc_p, fc_s)
    return tuple(np.ascontiguousarray(a) for a in out)


def program(nc, arrays, before):
    io = {k: nc.dram_tensor(k, a.shape, F32, kind="ExternalInput").ap() for k, a in arrays.items()}
    for k, shape in OUTS.items():
        io[k] = nc.dram_tensor(k, shape, F32, kind="ExternalOutput").ap()
    io["proj"] = nc.dram_tensor("proj", (IN_TILES, P, T), F32, kind="Internal").ap()
    with ExitStack() as ctx:
        return build(nc, io, ctx, before)


def kernel(**inputs):
    import concourse.bacc as bacc
    from concourse.bass_utils import run_bass_kernel_spmd

    arrays = lay_out({k: np.asarray(a) for k, a in inputs.items()})
    before = program(bacc.Bacc("TRN2", target_bir_lowering=False, num_devices=1), arrays, None)
    nc = bacc.Bacc("TRN2", target_bir_lowering=False, num_devices=1)
    program(nc, arrays, before)
    r = run_bass_kernel_spmd(nc, [arrays], core_ids=[0]).results[0]
    return give_back({k: r[k] for k in OUTS})
```
